# Optimizing a Trainium2 kernel written in Bass

```python
import jax
import jax.numpy as jnp
from jax import lax
import numpy as np

D_MODEL = 1024
BATCH = 1
SEQ = 512
DEPTH = 1

RET_HEADS = 4
RET_DK = 256
RET_DV = 512
RET_QK = RET_HEADS * RET_DK
RET_V = RET_HEADS * RET_DV
RET_CHUNK = 128
ROPE_BASE = 10000.0

LRU_WIDTH = 1536
LRU_BLOCKS = 8
LRU_BLOCK = LRU_WIDTH // LRU_BLOCKS
CONV_WIDTH = 4
LRU_C = 8.0

N_GROUPS = 4
EXPERTS_PER_GROUP = 8
N_EXPERTS = N_GROUPS * EXPERTS_PER_GROUP
TOP_K = 2
D_EXPERT = 512
MOE_ROWS = 128

IN_WIDTHS = (RET_QK, RET_QK, RET_V, RET_V, LRU_WIDTH, LRU_WIDTH, 2 * D_MODEL)

LN_EPS = 1e-5
DEEPNORM_ALPHA = (2.0 * DEPTH) ** 0.25
DEEPNORM_BETA = (8.0 * DEPTH) ** -0.25

kernel_name = 'hybrid_retention_rglru_hmoe_deepnorm'

def _layer_norm(x, g, b):
    xf = x.astype(jnp.float32)
    mu = xf.mean(-1, keepdims=True)
    var = jnp.square(xf - mu).mean(-1, keepdims=True)
    return ((xf - mu) * lax.rsqrt(var + LN_EPS) * g + b).astype(x.dtype)

def _head_norm(t):
    mu = t.mean(-1, keepdims=True)
    var = jnp.square(t - mu).mean(-1, keepdims=True)
    return (t - mu) * lax.rsqrt(var + LN_EPS)

def _rotary(t):
    S = t.shape[1]
    half = t.shape[-1] // 2
    inv = ROPE_BASE ** (-jnp.arange(half, dtype=jnp.float32) / half)
    ang = jnp.arange(S, dtype=jnp.float32)[:, None] * inv[None, :]
    cos = jnp.cos(ang)[None, :, None, :]
    sin = jnp.sin(ang)[None, :, None, :]
    t1, t2 = t[..., :half], t[..., half:]
    return jnp.concatenate([t1 * cos - t2 * sin, t1 * sin + t2 * cos], axis=-1)

def _retention(q, k, v):
    B, S, H, DK = q.shape
    DV = v.shape[-1]
    C = RET_CHUNK
    NC = S // C
    log_g = jnp.log1p(-(2.0 ** (-5.0 - jnp.arange(H, dtype=jnp.float32))))
    pos = jnp.arange(C, dtype=jnp.float32)
    diff = pos[:, None] - pos[None, :]
    causal = diff >= 0
    d_mask = jnp.where(causal[None], jnp.exp(log_g[:, None, None] * jnp.where(causal, diff, 0.0)[None]), 0.0)
    xi = jnp.exp(log_g[:, None] * (pos + 1.0)[None])
    zeta = jnp.exp(log_g[:, None] * (C - 1.0 - pos)[None])
    chunk_decay = jnp.exp(log_g * C)
    k = k * (DK ** -0.5)

    def to_chunks(t):
        return t.reshape(B, NC, C, H, t.shape[-1]).transpose(1, 0, 3, 2, 4)

    qc, kc, vc = to_chunks(q), to_chunks(k), to_chunks(v)

    def step(state, inp):
        qi, ki, vi = inp
        scores = jnp.einsum('bhnd,bhmd->bhnm', qi, ki) * d_mask
        inner = jnp.einsum('bhnm,bhme->bhne', scores, vi)
        cross = jnp.einsum('bhnd,bhde->bhne', qi, state) * xi[None, :, :, None]
        new_state = state * chunk_decay[None, :, None, None] + jnp.einsum(
            'bhmd,bhme->bhde', ki * zeta[None, :, :, None], vi)
        return new_state, inner + cross

    state0 = jnp.zeros((B, H, DK, DV), jnp.float32)
    _, out = lax.scan(step, state0, (qc, kc, vc))
    return out.transpose(1, 0, 3, 2, 4).reshape(B, S, H, DV)

def _causal_conv(u, w, b):
    out = lax.conv_general_dilated(
        u, w[:, None, :].astype(u.dtype), window_strides=(1,), padding=[(CONV_WIDTH - 1, 0)],
        dimension_numbers=('NWC', 'WIO', 'NWC'), feature_group_count=u.shape[-1])
    return out + b

def _rg_lru(u, w_r, b_r, w_i, b_i, lam):
    B, S, W = u.shape
    ub = u.reshape(B, S, LRU_BLOCKS, LRU_BLOCK)
    r = jax.nn.sigmoid(jnp.einsum('bsnc,ncd->bsnd', ub, w_r).reshape(B, S, W) + b_r)
    i = jax.nn.sigmoid(jnp.einsum('bsnc,ncd->bsnd', ub, w_i).reshape(B, S, W) + b_i)
    log_a = -LRU_C * r * jax.nn.softplus(-lam.astype(jnp.float32))
    a = jnp.exp(log_a)
    inp = jnp.sqrt(-jnp.expm1(2.0 * log_a)) * (i * u)

    def combine(left, right):
        a1, b1 = left
        a2, b2 = right
        return a1 * a2, a2 * b1 + b2

    _, h = lax.associative_scan(combine, (a, inp), axis=1)
    return h

def _hier_moe(x, w_group, b_group, w_exp_router, b_exp_router, w_e_gate, w_e_up, w_e_down):
    B, S, D = x.shape
    N = B * S
    xt = x.reshape(N, D)
    rows = jnp.arange(N)
    g_logits = (xt @ w_group + b_group).astype(jnp.float32)
    g_prob = jax.nn.softmax(g_logits, axis=-1)
    g_idx = jnp.argmax(g_logits, axis=-1)
    g_w = g_prob[rows, g_idx]
    e_logits = (xt @ w_exp_router + b_exp_router).astype(jnp.float32)
    e_logits = e_logits.reshape(N, N_GROUPS, EXPERTS_PER_GROUP)[rows, g_idx]
    top_v, top_i = lax.top_k(e_logits, TOP_K)
    weights = g_w[:, None] * jax.nn.softmax(top_v, axis=-1)
    expert = g_idx[:, None] * EXPERTS_PER_GROUP + top_i

    M = N * TOP_K
    flat_e = expert.reshape(M)
    flat_w = weights.reshape(M)
    flat_tok = jnp.repeat(rows, TOP_K)
    order = jnp.argsort(flat_e)
    se = flat_e[order]
    counts = jnp.zeros((N_EXPERTS,), jnp.int32).at[flat_e].add(1)
    padded = (counts + MOE_ROWS - 1) // MOE_ROWS * MOE_ROWS
    starts = jnp.cumsum(counts) - counts
    pad_ends = jnp.cumsum(padded)
    pad_starts = pad_ends - padded
    dest = pad_starts[se] + jnp.arange(M) - starts[se]
    n_groups_rows = -(-(M + N_EXPERTS * (MOE_ROWS - 1)) // MOE_ROWS)
    m_pad = n_groups_rows * MOE_ROWS
    row_tok = jnp.full((m_pad,), N, jnp.int32).at[dest].set(flat_tok[order])
    row_w = jnp.zeros((m_pad,), jnp.float32).at[dest].set(flat_w[order])
    group_e = jnp.minimum(
        jnp.searchsorted(pad_ends, jnp.arange(n_groups_rows) * MOE_ROWS, side='right'), N_EXPERTS - 1)
    x_rows = jnp.concatenate([xt, jnp.zeros((1, D), xt.dtype)], axis=0)[row_tok]
    x_rows = x_rows.reshape(n_groups_rows, MOE_ROWS, D)

    def expert_rows(args):
        xb, e = args
        h = jax.nn.silu(xb @ w_e_gate[e]) * (xb @ w_e_up[e])
        return h @ w_e_down[e]

    y_rows = lax.map(expert_rows, (x_rows, group_e)).reshape(m_pad, D)
    y = jax.ops.segment_sum(y_rows * row_w[:, None].astype(y_rows.dtype), row_tok, num_segments=N + 1)[:N]
    return y.reshape(B, S, D)

def _layer(x, w_in, b_merge, conv_w, conv_b, w_rg_r, b_rg_r, w_rg_i, b_rg_i, lru_lambda,
           w_ret_o, w_lru_o, w_out, ln1_g, ln1_b, w_group, b_group, w_exp_router, b_exp_router,
           w_e_gate, w_e_up, w_e_down, ln2_g, ln2_b):
    B, S, D = x.shape
    f32 = jnp.float32
    splits = [int(s) for s in np.cumsum(IN_WIDTHS)[:-1]]
    q, k, v, g, u_lru, gate_lru, gate_logits = jnp.split(x @ w_in, splits, axis=-1)

    q = _rotary(q.astype(f32).reshape(B, S, RET_HEADS, RET_DK))
    k = _rotary(k.astype(f32).reshape(B, S, RET_HEADS, RET_DK))
    v = v.astype(f32).reshape(B, S, RET_HEADS, RET_DV)
    ret = _head_norm(_retention(q, k, v)).reshape(B, S, RET_V)
    ret = (jax.nn.silu(g.astype(f32)) * ret).astype(x.dtype)

    u = _causal_conv(u_lru, conv_w, conv_b)
    h = _rg_lru(u.astype(f32), w_rg_r, b_rg_r, w_rg_i, b_rg_i, lru_lambda)
    lru = (jax.nn.gelu(gate_lru.astype(f32)) * h).astype(x.dtype)

    gates = jax.nn.sigmoid((gate_logits + b_merge).astype(f32)).astype(x.dtype)
    gate_ret, gate_rec = jnp.split(gates, 2, axis=-1)
    merged = gate_ret * (ret @ w_ret_o) + gate_rec * (lru @ w_lru_o)
    x = _layer_norm(DEEPNORM_ALPHA * x + merged @ w_out, ln1_g, ln1_b)

    moe = _hier_moe(x, w_group, b_group, w_exp_router, b_exp_router, w_e_gate, w_e_up, w_e_down)
    return _layer_norm(DEEPNORM_ALPHA * x + moe, ln2_g, ln2_b)

def setup_inputs(seed: int = 0) -> dict:
    key = jax.random.key(seed)
    ks = jax.random.split(key, 32)
    f32 = jnp.float32
    D = D_MODEL
    L = DEPTH
    sd = D ** -0.5
    beta = DEEPNORM_BETA

    def nrm(k, shape, scale):
        return jax.random.normal(k, shape, f32) * scale

    x = nrm(ks[0], (BATCH, SEQ, D), 1.0)
    w_in = jnp.concatenate([
        nrm(ks[1], (L, D, RET_QK), sd),
        nrm(ks[2], (L, D, RET_QK), sd),
        nrm(ks[3], (L, D, RET_V), sd * beta),
        nrm(ks[4], (L, D, RET_V), sd),
        nrm(ks[5], (L, D, LRU_WIDTH), sd),
        nrm(ks[6], (L, D, LRU_WIDTH), sd),
        nrm(ks[7], (L, D, 2 * D), sd)], axis=-1)
    b_merge = nrm(ks[8], (L, 2 * D), 0.01)
    conv_w = nrm(ks[9], (L, CONV_WIDTH, LRU_WIDTH), CONV_WIDTH ** -0.5)
    conv_b = nrm(ks[10], (L, LRU_WIDTH), 0.01)
    w_rg_r = nrm(ks[11], (L, LRU_BLOCKS, LRU_BLOCK, LRU_BLOCK), LRU_BLOCK ** -0.5)
    b_rg_r = nrm(ks[12], (L, LRU_WIDTH), 0.01)
    w_rg_i = nrm(ks[13], (L, LRU_BLOCKS, LRU_BLOCK, LRU_BLOCK), LRU_BLOCK ** -0.5)
    b_rg_i = nrm(ks[14], (L, LRU_WIDTH), 0.01)
    a_c = jax.random.uniform(ks[15], (L, LRU_WIDTH), f32, 0.9, 0.999)
    a0 = a_c ** (1.0 / LRU_C)
    lru_lambda = jnp.log(a0) - jnp.log1p(-a0)
    w_ret_o = nrm(ks[16], (L, RET_V, D), beta * RET_V ** -0.5)
    w_lru_o = nrm(ks[17], (L, LRU_WIDTH, D), beta * LRU_WIDTH ** -0.5)
    w_out = nrm(ks[18], (L, D, D), beta * sd)
    ln1_g = 1.0 + nrm(ks[19], (L, D), 0.01)
    ln1_b = nrm(ks[20], (L, D), 0.01)
    w_group = nrm(ks[21], (L, D, N_GROUPS), sd)
    b_group = nrm(ks[22], (L, N_GROUPS), 0.01)
    w_exp_router = nrm(ks[23], (L, D, N_EXPERTS), sd)
    b_exp_router = nrm(ks[24], (L, N_EXPERTS), 0.01)
    w_e_gate = nrm(ks[25], (L, N_EXPERTS, D, D_EXPERT), sd)
    w_e_up = nrm(ks[26], (L, N_EXPERTS, D, D_EXPERT), beta * sd)
    w_e_down = nrm(ks[27], (L, N_EXPERTS, D_EXPERT, D), beta * D_EXPERT ** -0.5)
    ln2_g = 1.0 + nrm(ks[28], (L, D), 0.01)
    ln2_b = nrm(ks[29], (L, D), 0.01)
    return {'x': x, 'w_in': w_in, 'b_merge': b_merge, 'conv_w': conv_w, 'conv_b': conv_b,
            'w_rg_r': w_rg_r, 'b_rg_r': b_rg_r, 'w_rg_i': w_rg_i, 'b_rg_i': b_rg_i,
            'lru_lambda': lru_lambda, 'w_ret_o': w_ret_o, 'w_lru_o': w_lru_o, 'w_out': w_out,
            'ln1_g': ln1_g, 'ln1_b': ln1_b, 'w_group': w_group, 'b_group': b_group,
            'w_exp_router': w_exp_router, 'b_exp_router': b_exp_router, 'w_e_gate': w_e_gate,
            'w_e_up': w_e_up, 'w_e_down': w_e_down, 'ln2_g': ln2_g, 'ln2_b': ln2_b}

def reference(x, w_in, b_merge, conv_w, conv_b, w_rg_r, b_rg_r, w_rg_i, b_rg_i, lru_lambda,
              w_ret_o, w_lru_o, w_out, ln1_g, ln1_b, w_group, b_group, w_exp_router, b_exp_router,
              w_e_gate, w_e_up, w_e_down, ln2_g, ln2_b):
    for l in range(DEPTH):
        x = _layer(x, w_in[l], b_merge[l], conv_w[l], conv_b[l], w_rg_r[l], b_rg_r[l], w_rg_i[l],
                   b_rg_i[l], lru_lambda[l], w_ret_o[l], w_lru_o[l], w_out[l], ln1_g[l], ln1_b[l],
                   w_group[l], b_group[l], w_exp_router[l], b_exp_router[l], w_e_gate[l], w_e_up[l],
                   w_e_down[l], ln2_g[l], ln2_b[l])
    return x


_drawn_inputs = setup_inputs


def setup_inputs(seed=0):
    import zlib

    import numpy as np

    out = dict(_drawn_inputs(seed))
    spreads = {}
    factors = {'b_merge': 8.0,
     'conv_b': 8.0,
     'w_rg_r': 3.251,
     'b_rg_r': 58.734,
     'b_rg_i': 29.144,
     'ln1_g': 4.825,
     'ln1_b': 5.105,
     'b_group': 8.0,
     'b_exp_router': 8.0,
     'ln2_g': 30.074,
     'ln2_b': 32.138}
    for name, (base, spread) in spreads.items():
        noise = np.random.default_rng([zlib.crc32(name.encode()), seed]).standard_normal(out[name].shape)
        drawn = base * np.exp(spread * noise) if base else spread * noise
        out[name] = jnp.asarray(drawn.astype(out[name].dtype))
    for name, factor in factors.items():
        out[name] = (out[name] * factor).astype(out[name].dtype)
    return out
```

```python
from contextlib import ExitStack

import numpy as np

import concourse.bass as bass
from concourse import mybir

F32 = mybir.dt.float32
F32R = mybir.dt.float32r
BF16 = mybir.dt.bfloat16
I32 = mybir.dt.int32
ALU = mybir.AluOpType
ACT = mybir.ActivationFunctionType
AX = mybir.AxisListType.X
ds = bass.ds

P = 128
TOKENS, D = 512, 1024
TT = TOKENS // P
KD = D // P
HEADS, DK, DV = 4, 256, 512
WIDTH, BLOCK = 1536, 192
WT = WIDTH // P
GROUPS, PER_GROUP, EXPERTS, FE = 4, 8, 32, 512
OFF_Q, OFF_K, OFF_V = 0, HEADS * DK, 2 * HEADS * DK
OFF_G = OFF_V + HEADS * DV
OFF_U = OFF_G + HEADS * DV
OFF_GATE = OFF_U + WIDTH
OFF_MERGE = OFF_GATE + WIDTH
EPS = 1e-5
ALPHA = 2.0 ** 0.25
MAX_OVERFLOW = (2 * TOKENS) // P - 1
LIST_COLS = TT * EXPERTS
NO_ROW = 4096

V_CONV_W, V_CONV_B, V_BR, V_BI, V_LAM, V_MERGE, V_ROWS = 0, 48, 60, 72, 84, 96, 112

RING = 4
U_LRU = 0
U_GREC = U_LRU + 24
U_LO = U_GREC + 8
U_QK0 = U_LO + 16
U_HEAD = U_QK0 + 4
U_LAST = U_HEAD + 48
U_GRET = U_LAST + 8
U_RET3 = U_GRET + 8
U_OUT = U_RET3 + 4
U_END = U_OUT + 8

MRING, MSPLIT = 6, 3
M_LAST = 4 + 6 * (EXPERTS - 1)
M_END = M_LAST + 2


class Unit:

    def __init__(self, base, j=0, i=0, per=0, ring=RING):
        assert per % ring == 0
        self.at = (base, i, per, ring)
        self.n = base + j + per * i
        self.j = j
        self.slot = (base + j) % ring
        self.fill = (base + j) // ring + (per // ring) * i + 1

    def ahead(self, d):
        base, i, per, ring = self.at
        return Unit(base, self.j + d, i, per, ring)


class Steps:

    def __init__(self, eng, sem):
        self.eng, self.sem, self.done, self.more = eng, sem, 0, 0

    def __call__(self, ins):
        ins.then_inc(self.sem, 1)
        self.done += 1

    def wait(self):
        self.eng.wait_ge(self.sem, self.done + self.more)

    def enter(self, i, per):
        self.more, self.start, self.per = i * per, self.done, per

    def leave(self, times):
        assert self.done - self.start == self.per, (self.done - self.start, self.per)
        self.more, self.done = 0, self.start + self.per * times


def layer(nc, io, out):
    ctx = ExitStack()
    with ctx:
        BASE = 16896
        ctx.enter_context(nc.sbuf_tensor("fence", [P, 53000], F32))

        def at(name, kb, shape, dt=F32):
            return nc.alloc_sbuf_tensor_at(name, shape, dt, offset=BASE + int(kb * 1024))

        def sem(name):
            return ctx.enter_context(nc.semaphore(name))

        bank = ctx.enter_context(nc.psum_tensor("bank", [P, 8, 512], F32))

        xt_hi, xt_lo = at("xt_hi", 0, [P, KD, TOKENS], F32R), at("xt_lo", 16, [P, KD, TOKENS], F32R)
        raw = at("raw", 32, [P, RING, 1024])
        w_hi, w_lo = at("w_hi", 48, [P, RING, 1024], F32R), at("w_lo", 64, [P, RING, 1024], F32R)
        merge = at("merge", 80, [P, KD, TOKENS])
        x_rows = at("x_rows", 144, [P, TT, D])
        vec_rows = at("vec_rows", 160, [P, P])
        rg_raw, rg_hi = at("rg_raw", 80, [P, 2, 896]), at("rg_hi", 87, [P, 2, 896], F32R)
        rg_lo = at("rg_lo", 197, [P, 2, 896], F32R)
        lru_hi, lru_lo = at("lru_hi", 96, [P, WT, TOKENS], F32R), at("lru_lo", 120, [P, WT, TOKENS], F32R)
        u_ext = at("u_ext", 144, [P, 3, TOKENS + 4])
        conv = at("conv", 151, [P, 3, TOKENS])
        conv_hi, conv_lo = at("conv_hi", 157, [P, 3, TOKENS], F32R), at("conv_lo", 163, [P, 3, TOKENS], F32R)
        gelu = at("gelu", 169, [P, 3, TOKENS])
        r_t, i_t, s_t = at("r_t", 175, [P, 3, TOKENS]), at("i_t", 181, [P, 3, TOKENS]), at("s_t", 187, [P, 3, TOKENS])
        inv = at("inv", 193, [P, TOKENS])
        acc = at("acc", 96, [P, KD, TOKENS])
        p_hi, p_lo, p_f = at("p_hi", 112, [P, 1280], F32R), at("p_lo", 117, [P, 1280], F32R), at("p_f", 122, [P, 1280])
        ret_hi, ret_lo = at("ret_hi", 112, [P, 4, TOKENS], F32R), at("ret_lo", 120, [P, 4, TOKENS], F32R)
        qk_hi, qk_lo = at("qk_hi", 128, [P, 4, TOKENS], F32R), at("qk_lo", 136, [P, 4, TOKENS], F32R)
        v_hi, v_lo = at("v_hi", 144, [P, TT, DV], F32R), at("v_lo", 152, [P, TT, DV], F32R)
        normed = at("normed", 160, [P, TT, DV])
        gated = at("gated", 168, [P, 4, TOKENS])
        rope = at("rope", 176, [P, 2, TOKENS])
        decay = at("decay", 180, [P, HEADS, TOKENS])
        rope_a, rope_b = at("rope_a", 188, [P, TOKENS]), at("rope_b", 190, [P, TOKENS])
        rope_o = at("rope_o", 192, [P, 4, TOKENS])
        g_ret = at("g_ret", 176, [P, KD, TOKENS])
        mrg_hi, mrg_lo = at("mrg_hi", 160, [P, KD, TOKENS], F32R), at("mrg_lo", 176, [P, KD, TOKENS], F32R)
        wo_hi, wo_lo = at("wo_hi", 0, [P, KD, D], F32R), at("wo_lo", 128, [P, KD, D], F32R)
        ln1 = at("ln1", 32, [P, 2, D])
        x_res = at("x_res", 48, [P, TT, D])
        x2 = at("x2", 64, [P, TT, D])
        x2_t = at("x2_t", 192, [P, 2, D])
        m_hi, m_lo = at("m_hi", 0, [P, MSPLIT, 2048], F32R), at("m_lo", 24, [P, MSPLIT, 2048], F32R)
        m_raw = at("m_raw", 80, [P, MRING, 2048])
        xe_hi, xe_lo = at("xe_hi", 128, [P, KD, P], F32R), at("xe_lo", 132, [P, KD, P], F32R)
        xg = at("xg", 136, [P, D])
        y_sb = at("y_sb", 140, [P, D])
        silu, h_sb = at("silu", 144, [P, FE]), at("h_sb", 146, [P, FE])
        ht_hi, ht_lo = at("ht_hi", 148, [P, FE], F32R), at("ht_lo", 150, [P, FE], F32R)
        ln2 = at("ln2", 160, [P, 2, D])
        y_rows = at("y_rows", 80, [P, TT, 2 * D])
        c = [204.25]

        def small(name, cols, dt=F32, size=4):
            t = at(name, c[0], [P, cols], dt)
            c[0] += (cols * size + 31) // 32 * 32 / 1024
            return t

        ident = small("ident", P)
        vec = small("vec", V_ROWS)
        rate = small("rate", WT)
        cur = small("cur", 2 * 7 * 3)
        cur_v = cur[:, :].rearrange("p (b k j) -> p b k j", b=2, k=7)
        stats, mv = small("stats", 12), small("mv", 2)
        scale_v = small("scale_v", 3)
        wts = small("wts", 8)
        lists, lists_x = small("lists", LIST_COLS, I32), small("lists_x", LIST_COLS, I32)
        cur_rate = small("cur_rate", 12)
        x_idx, y_idx = small("x_idx", 1, I32), small("y_idx", 1, I32)
        ovf_row = small("ovf_row", 2 * 8 + 1, I32)
        assert c[0] <= 207.4, c[0]
        rt_kb = [200.0]

        def rt(name, shape, dt=F32, size=4):
            t = at(name, rt_kb[0], [P, shape], dt)
            rt_kb[0] += (shape * size + 31) // 32 * 32 / 1024
            return t

        logit = rt("logit", TT * 36)
        w_rt = rt("w_rt", KD * 36)
        b_rt = rt("b_rt", 36)
        iota_g, iota_e = rt("iota_g", 4), rt("iota_e", 8)
        hot_g, hot_1, hot_2, e8 = rt("hot_g", 16), rt("hot_1", 32), rt("hot_2", 32), rt("e8", 32)
        t32, red, res = rt("t32", 32), rt("red", 4), rt("res", 64)
        val = rt("val", 8, I32)
        assert rt_kb[0] <= 204.25
        ones_bf, tri_bf = at("ones_bf", 153.25, [P, P], BF16), at("tri_bf", 153.5, [P, P], BF16)
        masked, masked_e = at("masked", 154, [P, TT * 32]), at("masked_e", 159, [P, TT * 32])
        mem0, mem1 = at("mem0", 154.5, [P, TT * 32]), at("mem1", 155, [P, TT * 32])
        mem_bf = at("mem_bf", 155.5, [P, TT * 32], BF16)
        over = at("over", 156, [P, 96])
        over_r, over_s = at("over_r", 156.5, [P, 96]), at("over_s", 157, [P, 96])
        over_c = at("over_c", 157.5, [P, 96])
        ovf_col, part = at("ovf_col", 158, [P, 1]), at("part", 158.25, [P, 1])
        addr = at("addr", 158.5, [P, 8], I32)
        addr_f = at("addr_f", 158.75, [P, 16])

        x2_dram = nc.dram_tensor("x2_dram", [TOKENS, D], F32).ap()
        y_dram = nc.dram_tensor("y_dram", [2 * TOKENS, D], F32).ap()
        list_dram = nc.dram_tensor("list_dram", [P * LIST_COLS, 1], I32).ap()

        loaded = [sem(f"weights_loaded{k}") for k in range(RING)]
        hi_done, split_done, units_done = sem("hi_done"), sem("split_done"), sem("units_done")
        vec_in, x_in, vec_turned, vec_ready = sem("vec_in"), [sem(f"x_in{t}") for t in range(TT)], sem("vec_turned"), sem("vec_ready")
        ident_ok, xt_turned, xt_hi_ok, xt_split = sem("ident_ok"), sem("xt_turned"), sem("xt_hi_ok"), sem("xt_split")
        lam_e, rate_ok, pads_ok = sem("lam_e"), sem("rate_ok"), sem("pads_ok")
        rg_in, rg_hi_ok, rg_split, rg_done = sem("rg_in"), sem("rg_hi_ok"), sem("rg_split"), sem("rg_done")
        cur_ok, u_out, conv_ok, conv_hi_ok, conv_split = sem("cur_ok"), sem("u_out"), sem("conv_ok"), sem("conv_hi_ok"), sem("conv_split")
        gelu_ok, gates_ok, tanh_ok, decay_ok, sqrt_ok, tail_ok, lru_split = sem("gelu_ok"), sem("gates_ok"), sem("tanh_ok"), sem("decay_ok"), sem("sqrt_ok"), sem("tail_ok"), sem("lru_split")
        grec_ok, lo_ok = sem("grec_ok"), sem("lo_ok")
        tables_in = sem("tables_in")
        roped, qk_hi_ok, qk_split = sem("roped"), sem("qk_hi_ok"), sem("qk_split")
        v_hi_ok, v_split = sem("v_hi_ok"), sem("v_split")
        scored, masked_ok, p_hi_ok, p_split, pv_ok = sem("scored"), sem("masked_ok"), sem("p_hi_ok"), sem("p_split"), sem("pv_ok")
        silu_ok, var_ok, std_ok, rstd_ok, normed_ok = sem("silu_ok"), sem("var_ok"), sem("std_ok"), sem("rstd_ok"), sem("normed_ok")
        turned, retf_ok, ret_hi_ok, ret_split, ret_out = sem("turned"), sem("retf_ok"), sem("ret_hi_ok"), sem("ret_split"), sem("ret_out")
        gret_ok, acc_ok, merged, mrg_hi_ok, mrg_split = sem("gret_ok"), sem("acc_ok"), sem("merged"), sem("mrg_hi_ok"), sem("mrg_split")
        ln1_in, res_in = sem("ln1_in"), sem("res_in")
        proj_ok, z_ok, x2_var, x2_std, x2_ok = (sem(n) for n in ("proj_ok", "z_ok", "x2_var", "x2_std", "x2_ok"))
        x2_turned, x2t_ok, routed, x2_stored = sem("x2_turned"), sem("x2t_ok"), sem("routed"), sem("x2_stored")
        router_in, consts_ok = sem("router_in"), sem("consts_ok")
        dve_steps, pool_steps = sem("dve_steps"), sem("pool_steps")
        list_empty, exp_ok, members_ok, ranked, ovf_ok, ovf_turned, addr_ok = (sem(n) for n in ("list_empty", "exp_ok", "members_ok", "ranked", "ovf_ok", "ovf_turned", "addr_ok"))
        list_set, scattered, lists_in, idx_ok, ovf_ready, x2a_ok = (sem(n) for n in ("list_set", "scattered", "lists_in", "idx_ok", "ovf_ready", "x2a_ok"))
        m_loaded = [sem(f"m_loaded{k}") for k in range(MRING)]
        m_hi_ok, m_split_ok, m_done = sem("m_hi_ok"), sem("m_split_ok"), sem("m_done")
        xg_in, xe_turned, xe_hi_ok, xe_split = sem("xg_in"), sem("xe_turned"), sem("xe_hi_ok"), sem("xe_split")
        m_silu, h_ok, h_turned, ht_hi_ok, ht_split = sem("m_silu"), sem("h_ok"), sem("h_turned"), sem("ht_hi_ok"), sem("ht_split")
        y_ok, y_sent, y_free, marks, lists_x_ok = sem("y_ok"), sem("y_sent"), sem("y_free"), sem("marks"), sem("lists_x_ok")
        moe_done, rows_in, ln2_in = sem("moe_done"), [sem(f"rows_in{t}") for t in range(TT)], sem("ln2_in")
        f_var, f_std, f_ok, stored = (sem(n) for n in ("f_var", "f_std", "f_ok", "stored"))

        w_in = io["w_in"][0].rearrange("(k p) n -> p k n", p=P)
        w_lru = io["w_lru_o"][0].rearrange("(k p) n -> p k n", p=P)
        w_ret = io["w_ret_o"][0].rearrange("(k p) n -> p k n", p=P)
        w_out = io["w_out"][0].rearrange("(k p) n -> k p n", p=P)
        w_gate = io["w_e_gate"][0].rearrange("e (k p) n -> p e k n", p=P)
        w_up = io["w_e_up"][0].rearrange("e (k p) n -> p e k n", p=P)
        w_down = io["w_e_down"][0].rearrange("e (k p) n -> p e k n", p=P)
        x_view = io["x"][0].rearrange("(t p) d -> t p d", p=P)
        out_view = out[0].rearrange("(t p) d -> t p d", p=P)

        def row(v):
            return v.rearrange("a n -> (a n)").partition_broadcast(P)

        block = ctx.enter_context(nc.Block())

        @block.sync
        def _(sp):
            def load(u, dst_cols, src, k):
                sp.wait_ge(split_done, u.n + 1)
                dst = raw[:, u.slot, 0:dst_cols].rearrange("p (k n) -> p k n", k=k)
                sp.dma_start(dst, src).then_inc(loaded[u.slot], 16)

            def load_cols(u, col):
                load(u, 1024, w_in[:, :, ds(col, P)] if not isinstance(col, int) else w_in[:, :, col:col + P], KD)

            vectors = [("conv_w", V_CONV_W, 48), ("conv_b", V_CONV_B, 12), ("b_rg_r", V_BR, 12),
                       ("b_rg_i", V_BI, 12), ("lru_lambda", V_LAM, 12), ("b_merge", V_MERGE, 16)]
            for name, r, n in vectors:
                src = io[name][0]
                src = src.rearrange("k (t p) -> (k t) p", p=P) if name == "conv_w" else src.rearrange("(t p) -> t p", p=P)
                sp.dma_start(vec_rows[r:r + n, :], src).then_inc(vec_in, 16)

            def load_gates(s):
                sp.wait_ge(rg_split, s + 1)
                for g, w in enumerate((io["w_rg_r"][0], io["w_rg_i"][0])):
                    a = w[ds(2 * s, 1)].rearrange("a i o -> (a i) o")
                    b = w[ds(2 * s + 1, 1)].rearrange("a i o -> (a i) o")
                    sp.dma_start(rg_raw[:, g, 0:192], a[0:128, :]).then_inc(rg_in, 16)
                    sp.dma_start(rg_raw[0:64, g, 256:448], a[128:192, :]).then_inc(rg_in, 16)
                    sp.dma_start(rg_raw[64:128, g, 448:640], b[0:64, :]).then_inc(rg_in, 16)
                    sp.dma_start(rg_raw[:, g, 704:896], b[64:192, :]).then_inc(rg_in, 16)

            sp.wait_ge(pads_ok, 1)
            with sp.Fori(0, 2) as i:
                for half in range(2):
                    s = 2 * i + half
                    for j in range(3):
                        load_cols(Unit(U_LRU, 6 * half + j, i, 12), s * 384 + (OFF_U + P * j))
                    for j in range(3):
                        if j == 2:
                            load_gates(s)
                        load_cols(Unit(U_LRU, 6 * half + 3 + j, i, 12), s * 384 + (OFF_GATE + P * j))
            for k in range(KD):
                load_cols(Unit(U_GREC, k), OFF_MERGE + D + P * k)
            with sp.Fori(0, 4) as i:
                for cc in range(2):
                    for part_k in range(2):
                        load(Unit(U_LO, 2 * cc + part_k, i, 4), 768, w_lru[:, 6 * part_k:6 * part_k + 6, ds(i * 256 + cc * P, P)], 6)

            def load_qk(h, u):
                for j in range(4):
                    load_cols(u.ahead(j), h * DK + (OFF_Q + P * j if j < 2 else OFF_K + P * (j - 2)))

            def load_vg(h, u):
                for j in range(4):
                    load(u.ahead(j), 1024, w_in[:, 2 * j:2 * j + 2, ds(h * DV + OFF_V, DV)] if not isinstance(h, int)
                         else w_in[:, 2 * j:2 * j + 2, OFF_V + h * DV:OFF_V + h * DV + DV], 2)
                for j in range(4):
                    load_cols(u.ahead(4 + j), h * DV + (OFF_G + P * j))

            def load_ret(h, u):
                for j in range(4):
                    rows = w_ret[:, ds(4 * h, 4), 256 * j:256 * j + 256] if not isinstance(h, int) else w_ret[:, 4 * h:4 * h + 4, 256 * j:256 * j + 256]
                    load(u.ahead(j), 1024, rows, 4)

            sp.wait_ge(lru_split, WT + 3)
            sp.wait_ge(conv_split, WT)
            sp.dma_start(rope[:, :, :], io["rope"].rearrange("a p n -> p a n")).then_inc(tables_in, 16)
            sp.dma_start(decay[:, :, :], io["decay"].rearrange("h p n -> p h n")).then_inc(tables_in, 16)
            sp.wait_ge(rg_done, 24 + 6)
            w_rt_v = w_rt[:, :].rearrange("p (k n) -> p k n", k=KD)
            sp.dma_start(w_rt_v[:, :, 0:GROUPS], io["w_group"][0].rearrange("(k p) n -> p k n", p=P)).then_inc(router_in, 16)
            sp.dma_start(w_rt_v[:, :, GROUPS:36], io["w_exp_router"][0].rearrange("(k p) n -> p k n", p=P)).then_inc(router_in, 16)
            sp.dma_start(b_rt[:, 0:GROUPS], row(io["b_group"])).then_inc(router_in, 16)
            sp.dma_start(b_rt[:, GROUPS:36], row(io["b_exp_router"])).then_inc(router_in, 16)
            load_qk(0, Unit(U_QK0))
            with sp.Fori(0, HEADS - 1) as h:
                load_vg(h, Unit(U_HEAD, 0, h, 16))
                load_qk(h + 1, Unit(U_HEAD, 8, h, 16))
                load_ret(h, Unit(U_HEAD, 12, h, 16))
            load_vg(HEADS - 1, Unit(U_LAST))
            for k in range(KD):
                load_cols(Unit(U_GRET, k), OFF_MERGE + P * k)
            load_ret(HEADS - 1, Unit(U_RET3))
            for k in range(KD):
                u = Unit(U_OUT, k)
                sp.wait_ge(split_done, u.n + 1)
                sp.dma_start(raw[:, u.slot, :], w_out[k]).then_inc(loaded[u.slot], 16)

            sp.wait_ge(split_done, U_END + RING)
            sp.wait_ge(units_done, U_OUT + RING)
            sp.dma_start(ln1[:, 0, :], row(io["ln1_g"])).then_inc(ln1_in, 16)
            sp.dma_start(ln1[:, 1, :], row(io["ln1_b"])).then_inc(ln1_in, 16)
            sp.dma_start(x_res[:, :, :], io["x"][0].rearrange("(t p) d -> p t d", p=P)).then_inc(res_in, 16)

            sp.wait_ge(mrg_split, KD)

            def load_m(u, src):
                sp.wait_ge(m_split_ok, u.n + 1)
                k = 4 if src.shape[-1] == FE else 2
                sp.dma_start(m_raw[:, u.slot, :].rearrange("p (k n) -> p k n", k=k), src).then_inc(m_loaded[u.slot], 16)

            def expert(w, e, k0, k1):
                return w[:, ds(e, 1), k0:k1, :].rearrange("p e k n -> p (e k) n")

            def load_gate_up(e, u):
                for j, w in enumerate((w_gate, w_up)):
                    for half in range(2):
                        load_m(u.ahead(2 * j + half), expert(w, e, 4 * half, 4 * half + 4))

            def load_down(e, u):
                for half in range(2):
                    load_m(u.ahead(half), expert(w_down, e, 2 * half, 2 * half + 2))

            load_gate_up(0, Unit(0, ring=MRING))
            for t in range(TT):
                sp.wait_ge(x2_ok, t + 1)
                sp.dma_start(x2_dram[t * P:(t + 1) * P, :], x2[:, t, :]).then_inc(x2_stored, 16)
            sp.wait_ge(mrg_split, KD)
            sp.wait_ge(proj_ok, TT)
            sp.dma_start(ln2[:, 0, :], row(io["ln2_g"])).then_inc(ln2_in, 16)
            sp.dma_start(ln2[:, 1, :], row(io["ln2_b"])).then_inc(ln2_in, 16)
            sp.wait_ge(scattered, 16 * 8)
            sp.dma_start(lists[:, :], list_dram.rearrange("(p n) a -> p (n a)", p=P)).then_inc(lists_in, 16)
            with sp.Fori(0, EXPERTS - 1) as i:
                load_gate_up(i + 1, Unit(4, 0, i, 6, MRING))
                load_down(i, Unit(4, 4, i, 6, MRING))
            load_down(EXPERTS - 1, Unit(M_LAST, ring=MRING))
            sp.wait_ge(ovf_ready, 1)
            n_over = sp.value_load(ovf_row[0:1, 16:17], min_val=0, max_val=MAX_OVERFLOW)
            with sp.Fori(0, MAX_OVERFLOW) as j:
                with sp.If(n_over > j):
                    e = sp.value_load(ovf_row[0:1, ds(j + 8, 1)], min_val=0, max_val=EXPERTS - 1)
                    load_gate_up(e, Unit(M_END, 0, j, 6, MRING))
                    load_down(e, Unit(M_END, 4, j, 6, MRING))
            sp.wait_ge(moe_done, 1)
            for t in range(TT):
                sp.dma_start(y_rows[:, t, :], y_dram[2 * P * t:2 * P * (t + 1), :].rearrange("(p k) d -> p (k d)", k=2)).then_inc(rows_in[t], 16)
            for t in range(TT):
                sp.wait_ge(f_ok, t + 1)
                sp.dma_start(out_view[t], x2[:, t, :]).then_inc(stored, 16)
            sp.wait_ge(stored, 16 * TT)

        @block.gpsimd
        def _(pool):
            steps = Steps(pool, pool_steps)
            pool.memset(ident[:, :], 0.0).then_inc(ident_ok, 1)
            pool.wait_ge(ident_ok, 1)
            pool.affine_select(out=ident[:, :], in_=ident[:, :], compare_op=ALU.not_equal, fill=1.0, base=0,
                               pattern=[[-1, P]], channel_multiplier=1).then_inc(ident_ok, 1)
            pool.memset(rg_raw[:, :, :], 0.0).then_inc(pads_ok, 1)
            pool.memset(lists[:, :], NO_ROW).then_inc(list_set, 1)
            pool.wait_ge(list_set, 1)
            pool.dma_start(list_dram.rearrange("(p n) a -> p (n a)", p=P), lists[:, :]).then_inc(list_empty, 16)
            pool.wait_ge(ret_out, 8 * HEADS)
            for k in range(KD):
                pool.wait_ge(gret_ok, k + 1)
                steps(pool.tensor_tensor(acc[:, k, :], acc[:, k, :], g_ret[:, k, :], ALU.mult))
                steps.wait()
                pool.tensor_tensor(acc[:, k, :], acc[:, k, :], merge[:, k, :], ALU.add).then_inc(acc_ok, 1)
            pool.wait_ge(proj_ok, TT)
            pool.iota(iota_g[:, :], pattern=[[1, 4]], base=-4, channel_multiplier=0, allow_small_or_imprecise_dtypes=True)
            pool.iota(iota_e[:, :], pattern=[[1, 8]], base=-8, channel_multiplier=0, allow_small_or_imprecise_dtypes=True)
            pool.iota(part[:, :], pattern=[[1, 1]], base=0, channel_multiplier=1, allow_small_or_imprecise_dtypes=True)
            pool.iota(over_c[:, :], pattern=[[1, 96]], base=EXPERTS, channel_multiplier=0, allow_small_or_imprecise_dtypes=True)
            pool.iota(val[:, :], pattern=[[2 * P, TT], [1, 2]], base=0, channel_multiplier=2)
            pool.memset(xg[:, :], 0.0)
            pool.memset(ones_bf[:, :], 1.0).then_inc(pads_ok, 1)
            pool.wait_ge(pads_ok, 2)
            pool.affine_select(out=tri_bf[:, :], in_=ones_bf[:, :], compare_op=ALU.is_gt, fill=0.0, base=0,
                               pattern=[[1, P]], channel_multiplier=-1).then_inc(consts_ok, 1)
            last_x, last_y = pool.to_reg(TOKENS - 1), pool.to_reg(2 * TOKENS - 1)
            pool.wait_ge(list_empty, 16)
            pool.wait_ge(addr_ok, 1)
            for n in range(8):
                pool.indirect_dma_start(list_dram, bass.IndirectOffsetOnAxis(ap=addr[:, n:n + 1], axis=0), val[:, n:n + 1], None).then_inc(scattered, 16)

            def gather(col):
                steps(pool.tensor_copy(x_idx[:, :], lists_x[:, ds(col, 1)] if not isinstance(col, int) else lists_x[:, col:col + 1]))
                steps.wait()
                pool.sem_inc(marks, 1)
                pool.indirect_dma_start(xg[:, :], None, x2_dram, bass.IndirectOffsetOnAxis(ap=x_idx[:, :], axis=0),
                                        bounds_check=last_x, oob_is_err=False).then_inc(xg_in, 16)

            def scatter(col):
                steps(pool.tensor_copy(y_idx[:, :], lists[:, ds(col, 1)] if not isinstance(col, int) else lists[:, col:col + 1]))
                steps.wait()
                pool.sem_inc(marks, 1)
                pool.indirect_dma_start(y_dram, bass.IndirectOffsetOnAxis(ap=y_idx[:, :], axis=0), y_sb[:, :], None,
                                        bounds_check=last_y, oob_is_err=False).then_inc(y_sent, 16)

            def send(s, col):
                pool.wait_ge(y_ok, s + 2)
                pool.sem_inc(marks, 1)
                scatter(col)
                pool.wait_ge(y_sent, 16 * s + 16)
                pool.sem_inc(y_free, 1)

            pool.sem_inc(y_free, 1)
            pool.wait_ge(lists_x_ok, 1)
            pool.wait_ge(x2_stored, 16 * TT)
            gather(0)
            pool.wait_ge(xe_turned, 1)
            gather(1)
            pool.wait_ge(xe_turned, 2)
            gather(2)
            with pool.Fori(0, EXPERTS - 1) as i:
                steps.enter(i, 2)
                pool.wait_ge(xe_turned, i + 3)
                pool.sem_inc(marks, 1)
                gather(i + 3)
                send(i, i)
                steps.leave(EXPERTS - 1)
            send(EXPERTS - 1, EXPERTS - 1)
            pool.wait_ge(ovf_ready, 1)
            n_over = pool.value_load(ovf_row[0:1, 16:17], min_val=0, max_val=MAX_OVERFLOW)
            with pool.Fori(0, MAX_OVERFLOW) as j:
                steps.enter(j, 2)
                with pool.If(n_over > j):
                    col = pool.value_load(ovf_row[0:1, ds(j, 1)], min_val=0, max_val=LIST_COLS - 1)
                    pool.wait_ge(xe_turned, j + (EXPERTS + 1))
                    pool.wait_ge(xg_in, 16 * j + 16 * (EXPERTS + 2))
                    pool.sem_inc(marks, 1)
                    gather(col)
                    send(j + EXPERTS, col)
                steps.leave(MAX_OVERFLOW)
            pool.sem_inc(moe_done, 1)

        @block.scalar
        def _(act):
            def copy(dst, src):
                return act.activation(dst, src, ACT.Copy)

            def split_hi(u):
                act.wait_ge(loaded[u.slot], 16 * u.fill)
                act.wait_ge(units_done, u.n + 1)
                copy(w_hi[:, u.slot, :], raw[:, u.slot, :]).then_inc(hi_done, 1)

            def done(u):
                act.wait_ge(units_done, u.n + 1 + RING)

            act.sem_inc(tanh_ok, 3)
            act.sem_inc(sqrt_ok, 3)
            act.sem_inc(decay_ok, 3)
            for t in range(TT):
                act.dma_start(x_rows[:, t, :], x_view[t]).then_inc(x_in[t], 16)
            for k in range(KD):
                act.wait_ge(xt_turned, k + 1)
                copy(xt_hi[:, k, :], bank[:, k, :]).then_inc(xt_hi_ok, 1)
            for j in range(3):
                split_hi(Unit(U_LRU, j))
            act.wait_ge(lam_e, 1)
            act.activation(cur[:, 12:24], cur[:, 0:12], ACT.Exp, scale=-1.0).then_inc(lam_e, 1)

            def tail_gates(s, b):
                for j in range(3):
                    act.wait_ge(rg_done, 6 * s + 2 * j + 1 + 6)
                    act.activation(r_t[:, j, :], bank[:, j, :], ACT.Sigmoid, bias=cur_v[:, b, 5, j:j + 1]).then_inc(gates_ok, 1)
                    act.wait_ge(rg_done, 6 * s + 2 * j + 2 + 6)
                    act.activation(i_t[:, j, :], bank[:, (6, 7, 3)[j], :], ACT.Sigmoid, bias=cur_v[:, b, 6, j:j + 1]).then_inc(gates_ok, 1)

            def tail_decay(s, b):
                act.wait_ge(lru_split, 3 * s + 3)
                for j in range(3):
                    act.wait_ge(gates_ok, 6 * s + 2 * j + 1 + 6)
                    act.activation(s_t[:, j, :], r_t[:, j, :], ACT.Tanh, scale=cur_rate[:, 6 * b + j:6 * b + j + 1]).then_inc(tanh_ok, 1)
                for j in range(3):
                    act.wait_ge(tanh_ok, 3 * s + j + 1 + 3)
                    act.activation(r_t[:, j, :], r_t[:, j, :], ACT.Exp, scale=cur_rate[:, 6 * b + 3 + j:6 * b + 4 + j]).then_inc(decay_ok, 1)
                for j in range(3):
                    act.activation(s_t[:, j, :], s_t[:, j, :], ACT.Sqrt).then_inc(sqrt_ok, 1)

            def evict_u(s, b, j, u):
                done(u)
                act.wait_ge(tail_ok, 3 * s + j + 1)
                act.wait_ge(cur_ok, s + 1)
                copy(u_ext[:, j, 3:3 + TOKENS], bank[:, j, :])
                act.activation(conv[:, j, :], bank[:, j, :], ACT.Identity, bias=cur_v[:, b, 4, j:j + 1],
                               scale=cur_v[:, b, 3, j:j + 1]).then_inc(u_out, 1)

            with act.Fori(0, 2) as i:
                for half in range(2):
                    s = 2 * i + half
                    u = [Unit(U_LRU, 6 * half + j, i, 12) for j in range(6)]
                    split_hi(u[0].ahead(3))
                    if half:
                        tail_gates(s - 1, 0)
                        tail_decay(s - 1, 0)
                    else:
                        with act.If(i > 0):
                            tail_gates(s - 1, 1)
                            tail_decay(s - 1, 1)
                    split_hi(u[1].ahead(3))
                    split_hi(u[2].ahead(3))
                    evict_u(s, half, 0, u[0])
                    split_hi(u[3].ahead(3))
                    evict_u(s, half, 1, u[1])
                    evict_u(s, half, 2, u[2])
                    act.wait_ge(rg_in, 128 * s + 128)
                    act.wait_ge(rg_done, 6 * s + 6)
                    copy(rg_hi[:, :, :], rg_raw[:, :, :]).then_inc(rg_hi_ok, 1)
                    for j in range(3):
                        act.wait_ge(conv_ok, 3 * s + j + 1)
                        copy(conv_hi[:, j, :], conv[:, j, :]).then_inc(conv_hi_ok, 1)
                    split_hi(u[4].ahead(3))
                    for j in range(3):
                        if j == 2:
                            split_hi(u[5].ahead(3))
                        done(u[3 + j])
                        act.activation(gelu[:, j, :], bank[:, 3 + j, :], ACT.Gelu_apprx_tanh).then_inc(gelu_ok, 1)

            def grec(k):
                done(Unit(U_GREC, k))
                act.activation(merge[:, k, :], bank[:, 4 + k % 2, :], ACT.Sigmoid,
                               bias=vec[:, V_MERGE + KD + k:V_MERGE + KD + k + 1]).then_inc(grec_ok, 1)

            for k in range(KD):
                split_hi(Unit(U_GREC, k).ahead(3))
                if k == 0:
                    tail_gates(3, 1)
                    act.wait_ge(rg_split, 4 + 1)
                    act.wait_ge(rg_done, 24 + 6)
                if k == 1:
                    tail_decay(3, 1)
                grec(k)
            with act.Fori(0, 4) as i:
                for j in range(4):
                    split_hi(Unit(U_LO, j, i, 4).ahead(3))

            def hi_qk(h, a, b):
                for x in range(a, b):
                    act.wait_ge(roped, 4 * h + x + 1)
                    act.wait_ge(scored, 4 * h + 4)
                    copy(qk_hi[:, x, :], rope_o[:, x, :]).then_inc(qk_hi_ok, 1)

            def hi_ret(h):
                for j in range(4):
                    act.wait_ge(retf_ok, 4 * h + j + 1)
                    act.wait_ge(pv_ok, 4 * h + 8)
                    copy(ret_hi[:, j, :], gated[:, j, :]).then_inc(ret_hi_ok, 1)

            def act_qk(h, u, ret=None):
                for j in range(4):
                    split_hi(u.ahead(j + 3))
                    if j == 2:
                        hi_qk(h, 0, 2)
                        if ret is not None:
                            hi_ret(ret)
                hi_qk(h, 2, 4)

            def act_vg(h, u):
                for j in range(4):
                    split_hi(u.ahead(j + 3))
                done(u.ahead(3))
                act.wait_ge(pv_ok, 4 * h + 4)
                for t in range(TT):
                    copy(v_hi[:, t, :], bank[:, 4 + t, :]).then_inc(v_hi_ok, 1)
                at_p = 0
                for k in range(TT):
                    w = TOKENS - k * P
                    act.wait_ge(masked_ok, 4 * h + k + 1)
                    copy(p_hi[:, at_p:at_p + w], p_f[:, at_p:at_p + w]).then_inc(p_hi_ok, 1)
                    at_p += w
                act.wait_ge(ret_split, 4 * h + 4)
                for j in range(4):
                    split_hi(u.ahead(4 + j + 3))
                    done(u.ahead(4 + j))
                    act.activation(gated[:, j, :], bank[:, 4 + j, :], ACT.Silu).then_inc(silu_ok, 1)
                act.wait_ge(turned, 4 * h + 4)
                for t in range(TT):
                    act.wait_ge(var_ok, 4 * h + t + 1)
                    act.activation(scale_v[:, 0:1], mv[:, 1:2], ACT.Sqrt).then_inc(std_ok, 1)
                    act.wait_ge(rstd_ok, 4 * h + t + 1)
                    act.activation(normed[:, t, :], bank[:, t, :], ACT.Identity, bias=scale_v[:, 2:3], scale=scale_v[:, 1:2]).then_inc(normed_ok, 1)

            act_qk(0, Unit(U_QK0))
            with act.Fori(0, HEADS - 1) as h:
                act_vg(h, Unit(U_HEAD, 0, h, 16))
                act_qk(h + 1, Unit(U_HEAD, 8, h, 16), h)
                for j in range(4):
                    split_hi(Unit(U_HEAD, 12 + j, h, 16).ahead(3))
            act_vg(HEADS - 1, Unit(U_LAST))
            for k in range(KD):
                u = Unit(U_GRET, k)
                split_hi(u.ahead(3))
                done(u)
                act.wait_ge(p_split, 4 * HEADS)
                act.activation(g_ret[:, k, :], bank[:, k % 4, :], ACT.Sigmoid, bias=vec[:, V_MERGE + k:V_MERGE + k + 1]).then_inc(gret_ok, 1)
                if k == 3:
                    hi_ret(HEADS - 1)

            def split_out_hi(n):
                if n < U_OUT:
                    return split_hi(Unit(n))
                u = Unit(n)
                act.wait_ge(loaded[u.slot], 16 * u.fill)
                act.wait_ge(units_done, U_RET3 + RING)
                copy(wo_hi[:, n - U_OUT, :], raw[:, u.slot, :]).then_inc(hi_done, 1)

            nxt = U_RET3 + 3
            for j in range(4):
                for _ in range(3 if j == 0 else 2):
                    split_out_hi(nxt)
                    nxt += 1
                for k in (2 * j, 2 * j + 1):
                    act.wait_ge(merged, k + 1)
                    act.wait_ge(ret_split, 4 * HEADS + 4)
                    act.wait_ge(turned, 4 * HEADS + 4)
                    copy(mrg_hi[:, k, :], acc[:, k, :]).then_inc(mrg_hi_ok, 1)
            assert nxt == U_END

            def x2t_out(t):
                act.wait_ge(x2_turned, t + 1)
                if t >= 2:
                    act.wait_ge(routed, t - 1)
                if t == 0:
                    act.wait_ge(qk_split, 4 * HEADS)
                copy(x2_t[:, t % 2, :].rearrange("p (b n) -> p b n", b=2), bank[:, 4:6, :]).then_inc(x2t_ok, 1)

            for t in range(TT):
                if t:
                    x2t_out(t - 1)
                act.wait_ge(x2_var, t + 1)
                act.activation(scale_v[:, 0:1], mv[:, 1:2], ACT.Sqrt).then_inc(x2_std, 1)
            x2t_out(TT - 1)
            act.wait_ge(exp_ok, 1)
            act.activation(res[:, 8:28], res[:, 8:28], ACT.Exp).then_inc(exp_ok, 1)
            act.wait_ge(x2_stored, 16 * TT)
            for t in range(TT):
                act.activation(x2[:, t, :], x2[:, t, :], ACT.Copy, scale=ALPHA).then_inc(x2a_ok, 1)

            def m_hi_part(u):
                act.wait_ge(m_loaded[u.slot], 16 * u.fill)
                act.wait_ge(m_done, u.n + 1)
                copy(m_hi[:, u.slot % MSPLIT, :], m_raw[:, u.slot, :]).then_inc(m_hi_ok, 1)

            def m_finished(u):
                act.wait_ge(m_done, u.n + 1 + MSPLIT)

            def xe_hi_part(s):
                act.wait_ge(xe_turned, s + 1)
                copy(xe_hi[:, :, :].rearrange("p (b k) n -> p b (k n)", b=2), bank[:, 4:6, :]).then_inc(xe_hi_ok, 1)

            def ht_hi_part(s):
                act.wait_ge(h_turned, s + 1)
                copy(ht_hi[:, :], bank[:, 6, :]).then_inc(ht_hi_ok, 1)

            def silu_part(s, u):
                m_finished(u)
                act.activation(silu[:, :], bank[:, 0, :], ACT.Silu).then_inc(m_silu, 1)

            def y_out(s, u):
                m_finished(u)
                act.wait_ge(y_free, s + 1)
                copy(y_sb[:, :].rearrange("p (b n) -> p b n", b=2), bank[:, 2:4, :]).then_inc(y_ok, 1)

            u = Unit(0, ring=MRING)
            act.wait_ge(proj_ok, TT)
            act.wait_ge(consts_ok, 1)
            m_hi_part(u)
            m_hi_part(u.ahead(1))
            xe_hi_part(0)
            for j in range(4):
                if j == 2:
                    silu_part(0, u.ahead(1))
                m_hi_part(u.ahead(j + 2))
            xe_hi_part(1)
            with act.Fori(0, EXPERTS - 1) as i:
                u = Unit(4, 0, i, 6, MRING)
                m_hi_part(u.ahead(2))
                ht_hi_part(i)
                m_hi_part(u.ahead(3))
                m_hi_part(u.ahead(4))
                silu_part(i + 1, u.ahead(1))
                m_hi_part(u.ahead(5))
                m_hi_part(u.ahead(6))
                xe_hi_part(i + 2)
                m_hi_part(u.ahead(7))
                y_out(i, u.ahead(5))
            ht_hi_part(EXPERTS - 1)
            y_out(EXPERTS - 1, Unit(M_LAST, 1, ring=MRING))
            act.wait_ge(ovf_ready, 1)
            n_over = act.value_load(ovf_row[0:1, 16:17], min_val=0, max_val=MAX_OVERFLOW)
            with act.Fori(0, MAX_OVERFLOW) as j:
                with act.If(n_over > j):
                    u = Unit(M_END, 0, j, 6, MRING)
                    xe_hi_part(j + (EXPERTS + 1))
                    for k in range(4):
                        m_hi_part(u.ahead(k))
                    silu_part(j + EXPERTS, u.ahead(1))
                    ht_hi_part(j + EXPERTS)
                    m_hi_part(u.ahead(4))
                    m_hi_part(u.ahead(5))
                    y_out(j + EXPERTS, u.ahead(5))
            for t in range(TT):
                act.wait_ge(f_var, t + 1)
                act.activation(scale_v[:, 0:1], mv[:, 1:2], ACT.Sqrt).then_inc(f_std, 1)

        @block.vector
        def _(dve):
            step = Steps(dve, dve_steps)

            def tt(dst, a, b, op):
                return dve.tensor_tensor(dst, a, b, op)

            def sub(dst, a, b_r):
                return dve.tensor_tensor(dst, a, b_r.bitcast(F32), ALU.subtract)

            def split_lo(u):
                dve.wait_ge(hi_done, u.n + 1)
                sub(w_lo[:, u.slot, :], raw[:, u.slot, :], w_hi[:, u.slot, :]).then_inc(split_done, 1)

            def done(u):
                dve.wait_ge(units_done, u.n + 1 + RING)

            dve.sem_inc(split_done, RING)
            dve.sem_inc(rg_split, 1)
            dve.sem_inc(tail_ok, 3)
            dve.sem_inc(lru_split, 3)
            dve.sem_inc(lo_ok, 2)
            dve.sem_inc(ret_split, 4)
            dve.sem_inc(ret_out, 8)
            dve.sem_inc(m_split_ok, MRING)
            dve.wait_ge(vec_turned, 1)
            dve.tensor_copy(vec[:, :], bank[:, 7, 0:V_ROWS]).then_inc(vec_ready, 1)
            for k in range(KD):
                dve.wait_ge(xt_hi_ok, k + 1)
                sub(xt_lo[:, k, :], bank[:, k, :], xt_hi[:, k, :]).then_inc(xt_split, 1)
            step(dve.memset(u_ext[:, :, 0:3], 0.0))
            step.wait()
            for j in range(3):
                split_lo(Unit(U_LRU, j))

            dve.wait_ge(vec_ready, 1)
            lam, mag, e, s, s2, q = vec[:, V_LAM:V_LAM + 12], cur[:, 0:12], cur[:, 12:24], cur[:, 24:36], inv[:, 0:12], inv[:, 12:24]
            neg = inv[:, 24:36]
            step(dve.tensor_scalar(neg, lam, -1.0, None, ALU.mult))
            step.wait()
            tt(mag, lam, neg, ALU.max).then_inc(lam_e, 1)
            dve.wait_ge(lam_e, 2)
            step(dve.tensor_scalar(q, e, 2.0, None, ALU.add))
            step.wait()
            step(dve.reciprocal(s, q))
            step.wait()
            step(tt(s, s, e, ALU.mult))
            step.wait()
            step(tt(s2, s, s, ALU.mult))
            step.wait()
            step(dve.tensor_scalar(q, s2, 1.0 / 19, None, ALU.mult))
            for k in range(8, 0, -1):
                step.wait()
                step(dve.scalar_tensor_tensor(q, q, 1.0 / (2 * k + 1), s2, ALU.add, ALU.mult))
            step.wait()
            step(dve.scalar_tensor_tensor(q, q, 1.0, s, ALU.add, ALU.mult))
            step(dve.tensor_scalar(neg, neg, 0.0, 4.0, ALU.max, ALU.mult))
            step.wait()
            dve.scalar_tensor_tensor(rate[:, :], q, 8.0, neg, ALU.mult, ALU.add).then_inc(rate_ok, 1)
            dve.wait_ge(rate_ok, 1)

            def tail(s, j):
                r, iv, sq = r_t[:, j, :], i_t[:, j, :], s_t[:, j, :]
                dve.wait_ge(gates_ok, 6 * s + 2 * j + 2 + 6)
                step(tt(iv, iv, conv[:, j, :], ALU.mult))
                dve.wait_ge(sqrt_ok, 3 * s + j + 1 + 3)
                dve.wait_ge(decay_ok, 3 * s + j + 1 + 3)
                step(dve.scalar_tensor_tensor(sq, r, 1.0, sq, ALU.add, ALU.mult))
                step.wait()
                step(tt(iv, iv, sq, ALU.mult))
                step.wait()
                step(dve.tensor_tensor_scan(sq, r, iv, 0.0, ALU.mult, ALU.add))
                step.wait()
                dve.wait_ge(gelu_ok, 3 * s + j + 1 + 3)
                tt(sq, sq, gelu[:, j, :], ALU.mult).then_inc(tail_ok, 1)

            def lru_parts(s):
                dve.wait_ge(tail_ok, 3 * s + 6)
                if not isinstance(s, int):
                    s = nc.s_assert_within(s, 0, 3, skip_runtime_bounds_check_because="runs for blocks 0 to 3 only")
                for j in range(3):
                    k = 3 * s + j
                    at_k = slice(k, k + 1) if isinstance(k, int) else ds(k, 1)
                    h, lo = lru_hi[:, at_k, :].rearrange("p a n -> p (a n)"), lru_lo[:, at_k, :].rearrange("p a n -> p (a n)")
                    step(dve.tensor_scalar(h, s_t[:, j, :], 1.0, None, ALU.mult))
                    step.wait()
                    sub(lo, s_t[:, j, :], h).then_inc(lru_split, 1)

            def conv_tile(s, b, j):
                dve.wait_ge(u_out, 3 * s + j + 1)
                for tap in (2, 1):
                    step(dve.scalar_tensor_tensor(conv[:, j, :], u_ext[:, j, tap:tap + TOKENS], cur_v[:, b, tap, j:j + 1],
                                                  conv[:, j, :], ALU.mult, ALU.add))
                    step.wait()
                dve.scalar_tensor_tensor(conv[:, j, :], u_ext[:, j, 0:TOKENS], cur_v[:, b, 0, j:j + 1],
                                         conv[:, j, :], ALU.mult, ALU.add).then_inc(conv_ok, 1)

            vec_k = vec[:, 0:84].rearrange("p (k t) -> p k t", t=WT)

            def block_vectors(s, b):
                step(dve.tensor_scalar(cur_rate[:, 6 * b:6 * b + 3], rate[:, ds(3 * s, 3)], 1.0, None, ALU.mult))
                step(dve.tensor_scalar(cur_rate[:, 6 * b + 3:6 * b + 6], rate[:, ds(3 * s, 3)], -2.0, None, ALU.mult))
                step.wait()
                dve.tensor_scalar(cur_v[:, b, :, :], vec_k[:, :, ds(3 * s, 3)], 1.0, None, ALU.mult).then_inc(cur_ok, 1)

            def lru_slots(i, half):
                s = 2 * i + half
                u = [Unit(U_LRU, 6 * half + j, i, 12) for j in range(6)]
                split_lo(u[0].ahead(3))
                block_vectors(s, half)
                for j in range(3):
                    if half:
                        tail(s - 1, j)
                    else:
                        with dve.If(i > 0):
                            before = step.done
                            tail(s - 1, j)
                        with dve.Else():
                            dve.sem_inc(dve_steps, step.done - before)
                    split_lo(u[1 + j].ahead(3))
                    if j == 1:
                        dve.wait_ge(cur_ok, s + 1)
                        conv_tile(s, half, 0)
                conv_tile(s, half, 1)
                conv_tile(s, half, 2)
                dve.wait_ge(rg_hi_ok, s + 1)
                sub(rg_lo[:, :, :], rg_raw[:, :, :], rg_hi[:, :, :]).then_inc(rg_split, 1)
                for j in range(3):
                    dve.wait_ge(conv_hi_ok, 3 * s + j + 1)
                    sub(conv_lo[:, j, :], conv[:, j, :], conv_hi[:, j, :]).then_inc(conv_split, 1)
                split_lo(u[4].ahead(3))
                split_lo(u[5].ahead(3))
                if half:
                    lru_parts(s - 1)
                else:
                    with dve.If(i > 0):
                        before = step.done
                        lru_parts(s - 1)
                    with dve.Else():
                        dve.sem_inc(dve_steps, step.done - before)

            per = 2 * (2 + 3 * 4 + 3 * 2 + 3)
            with dve.Fori(0, 2) as i:
                step.enter(i, per)
                lru_slots(i, 0)
                lru_slots(i, 1)
                step.leave(2)
            for k in range(KD):
                split_lo(Unit(U_GREC, k).ahead(3))
                if 1 <= k <= 3:
                    tail(3, k - 1)
                if k == 4:
                    lru_parts(3)
            dve.wait_ge(grec_ok, KD)
            with dve.Fori(0, 4) as i:
                for cc in range(2):
                    for j in range(2):
                        split_lo(Unit(U_LO, 2 * cc + j, i, 4).ahead(3))
                    done(Unit(U_LO, 2 * cc + 1, i, 4))
                    m = merge[:, ds(2 * i + cc, 1), :].rearrange("p a n -> p (a n)")
                    tt(m, m, bank[:, cc, :], ALU.mult).then_inc(lo_ok, 1)

            def rotate(h, a):
                cos, sin = rope[:, 0, :], rope[:, 1, :]
                for x, (f, g, op) in enumerate(((cos, sin, ALU.subtract), (sin, cos, ALU.add))):
                    if not (isinstance(h, int) and h == 0 and a + x == 0):
                        dve.wait_ge(roped, 4 * h + a + x)
                    step(tt(rope_a[:, :], bank[:, a, :], f, ALU.mult))
                    step(tt(rope_b[:, :], bank[:, a + 1, :], g, ALU.mult))
                    step.wait()
                    tt(rope_o[:, a + x, :], rope_a[:, :], rope_b[:, :], op).then_inc(roped, 1)

            def lo_qk(h, a):
                for x in (a, a + 1):
                    dve.wait_ge(qk_hi_ok, 4 * h + x + 1)
                    sub(qk_lo[:, x, :], rope_o[:, x, :], qk_hi[:, x, :]).then_inc(qk_split, 1)

            def ret_turned(h):
                for j in range(4):
                    dve.wait_ge(turned, 4 * h + j + 1 + 4)
                    tt(gated[:, j, :], bank[:, 4 + j, :], gated[:, j, :], ALU.mult).then_inc(retf_ok, 1)

            def lo_ret(h):
                for j in range(4):
                    dve.wait_ge(ret_hi_ok, 4 * h + j + 1)
                    sub(ret_lo[:, j, :], gated[:, j, :], ret_hi[:, j, :]).then_inc(ret_split, 1)

            def dve_qk(h, u, ret=None):
                split_lo(u.ahead(3))
                split_lo(u.ahead(4))
                done(u.ahead(1))
                if ret is None:
                    step(dve.memset(acc[:, :, :], 0.0))
                    step.wait()
                rotate(h, 0)
                split_lo(u.ahead(5))
                lo_qk(h, 0)
                if ret is not None:
                    ret_turned(ret)
                    lo_ret(ret)
                split_lo(u.ahead(6))
                done(u.ahead(3))
                rotate(h, 2)
                lo_qk(h, 2)

            def dve_vg(h, u):
                for j in range(4):
                    split_lo(u.ahead(j + 3))
                for t in range(TT):
                    dve.wait_ge(v_hi_ok, 4 * h + t + 1)
                    sub(v_lo[:, t, :], bank[:, 4 + t, :], v_hi[:, t, :]).then_inc(v_split, 1)
                d = decay[:, h, :] if isinstance(h, int) else decay[:, ds(h, 1), :].rearrange("p a n -> p (a n)")
                spans, at_p = [], 0
                for k in range(TT):
                    spans.append((at_p, at_p + TOKENS - k * P))
                    at_p = spans[-1][1]
                for k, (a, b) in enumerate(spans):
                    dve.wait_ge(scored, 4 * h + k + 1 + 4)
                    tt(p_f[:, a:b], bank[:, k, 0:b - a], d[:, 0:b - a], ALU.mult).then_inc(masked_ok, 1)
                for k, (a, b) in enumerate(spans):
                    dve.wait_ge(p_hi_ok, 4 * h + k + 1)
                    sub(p_lo[:, a:b], p_f[:, a:b], p_hi[:, a:b]).then_inc(p_split, 1)
                for j in range(4):
                    split_lo(u.ahead(4 + j + 3))
                for t in range(TT):
                    dve.wait_ge(pv_ok, 4 * h + t + 1 + 4)
                    moments([bank[:, t, :]], var_ok, std_ok, rstd_ok, 4 * h + t + 1)

            def moments(parts, var, std, rstd, n):
                for x, part_ap in enumerate(parts):
                    step(dve.bn_stats(stats[:, 6 * x:6 * x + 6], part_ap))
                step.wait()
                dve.sem_inc(marks, 1)
                step(dve.bn_aggr(mv[:, :], stats[:, 0:6 * len(parts)]))
                step.wait()
                dve.tensor_scalar(mv[:, 1:2], mv[:, 1:2], EPS, None, ALU.add).then_inc(var, 1)
                dve.wait_ge(std, n)
                step(dve.reciprocal(scale_v[:, 1:2], scale_v[:, 0:1]))
                step.wait()
                dve.scalar_tensor_tensor(scale_v[:, 2:3], mv[:, 0:1], -1.0, scale_v[:, 1:2], ALU.mult, ALU.mult).then_inc(rstd, 1)
                dve.wait_ge(rstd, n)

            dve.wait_ge(tables_in, 32)
            dve_qk(0, Unit(U_QK0))
            per = 4 * 3 + 8
            with dve.Fori(0, HEADS - 1) as h:
                step.enter(h, per)
                dve_vg(h, Unit(U_HEAD, 0, h, 16))
                dve_qk(h + 1, Unit(U_HEAD, 8, h, 16), h)
                for j in range(4):
                    u = Unit(U_HEAD, 12 + j, h, 16)
                    split_lo(u.ahead(3))
                    done(u)
                    for k in (2 * j, 2 * j + 1):
                        dve.wait_ge(ret_out, 8 * h + k + 1)
                        tt(acc[:, k, :], acc[:, k, :], bank[:, 4 + k % 4, :], ALU.add).then_inc(ret_out, 1)
                step.leave(HEADS - 1)
            dve_vg(HEADS - 1, Unit(U_LAST))
            for k in range(KD):
                split_lo(Unit(U_GRET, k).ahead(3))
                if k == 3:
                    ret_turned(HEADS - 1)
                if k == 4:
                    lo_ret(HEADS - 1)

            def split_out_lo(n):
                u = Unit(n)
                dve.wait_ge(hi_done, n + 1)
                if n < U_OUT:
                    sub(w_lo[:, u.slot, :], raw[:, u.slot, :], w_hi[:, u.slot, :]).then_inc(split_done, 1)
                else:
                    sub(wo_lo[:, n - U_OUT, :], raw[:, u.slot, :], wo_hi[:, n - U_OUT, :]).then_inc(split_done, 1)

            nxt = U_RET3 + 3
            dve.wait_ge(gret_ok, KD)
            for j in range(4):
                for _ in range(3 if j == 0 else 2):
                    split_out_lo(nxt)
                    nxt += 1
                done(Unit(U_RET3 + j))
                pair = (2 * j, 2 * j + 1)
                for k in pair:
                    dve.wait_ge(acc_ok, k + 1)
                    tt(g_ret[:, k, :], g_ret[:, k, :], bank[:, 4 + k % 4, :], ALU.mult).then_inc(ret_out, 1)
                for k in pair:
                    dve.wait_ge(ret_out, 8 * HEADS + k + 1)
                    tt(acc[:, k, :], acc[:, k, :], g_ret[:, k, :], ALU.add).then_inc(merged, 1)
                for k in pair:
                    dve.wait_ge(mrg_hi_ok, k + 1)
                    sub(mrg_lo[:, k, :], acc[:, k, :], mrg_hi[:, k, :]).then_inc(mrg_split, 1)

            dve.wait_ge(res_in, 16)
            dve.wait_ge(ln1_in, 32)

            def layer_norm(t, ln, var, std, ok):
                xt = x2[:, t, :]
                for half in range(2):
                    step(dve.bn_stats(stats[:, 6 * half:6 * half + 6], x2[:, t, 512 * half:512 * half + 512]))
                step.wait()
                step(dve.bn_aggr(mv[:, :], stats[:, :]))
                step.wait()
                dve.tensor_scalar(mv[:, 1:2], mv[:, 1:2], EPS, None, ALU.add).then_inc(var, 1)
                step(dve.scalar_tensor_tensor(xt, xt, mv[:, 0:1], ln[:, 0, :], ALU.subtract, ALU.mult))
                dve.wait_ge(std, t + 1)
                step(dve.reciprocal(scale_v[:, 1:2], scale_v[:, 0:1]))
                step.wait()
                dve.scalar_tensor_tensor(xt, xt, scale_v[:, 1:2], ln[:, 1, :], ALU.mult, ALU.add).then_inc(ok, 1)

            for t in range(TT):
                dve.wait_ge(proj_ok, t + 1)
                for half in range(2):
                    c0, c1 = 512 * half, 512 * half + 512
                    dve.scalar_tensor_tensor(x2[:, t, c0:c1], x_res[:, t, c0:c1], ALPHA, bank[:, 2 * (t % 2) + half, :],
                                             ALU.mult, ALU.add).then_inc(z_ok, 1)
                dve.wait_ge(z_ok, 2 * t + 2)
                layer_norm(t, ln1, x2_var, x2_std, x2_ok)

            dve.wait_ge(router_in, 64)
            dve.wait_ge(consts_ok, 1)
            dve.wait_ge(routed, TT)
            lg = logit[:, :].rearrange("p (t n) -> p t n", t=TT)
            step(tt(lg, bank[:, 6, 0:TT * 36].rearrange("p (t n) -> p t n", t=TT),
                    b_rt[:, :].unsqueeze(1).to_broadcast([P, TT, 36]), ALU.add))
            step.wait()

            def wide(ap, n):
                return ap.unsqueeze(2).to_broadcast([P, TT, n])

            def first_max(vals, n, iota, best, hot):
                v3 = vals
                h3 = hot.rearrange("p (t n) -> p t n", t=TT)
                step(dve.tensor_reduce(best, v3, AX, ALU.max))
                step.wait()
                step(tt(h3, v3, wide(best, n), ALU.is_ge))
                step.wait()
                it = iota[:, :].unsqueeze(1).to_broadcast([P, TT, n])
                step(tt(h3, h3, it, ALU.mult))
                step.wait()
                step(dve.tensor_reduce(red[:, :], h3, AX, ALU.min))
                step.wait()
                step(tt(h3, it, wide(red[:, :], n), ALU.is_equal))
                step.wait()

            best_g, best_1, best_2 = res[:, 0:4], res[:, 4:8], res[:, 28:32]
            diff, exps = res[:, 8:12], res[:, 12:28]
            first_max(lg[:, :, 0:4], 4, iota_g, best_g, hot_g[:, :])
            step(tt(exps.rearrange("p (t n) -> p t n", t=TT), lg[:, :, 0:4], wide(best_g, 4), ALU.subtract))
            m4 = masked[:, :].rearrange("p (t g e) -> p t g e", t=TT, g=GROUPS)
            hg = hot_g[:, :].rearrange("p (t g) -> p t g", t=TT)
            for t in range(TT):
                step(tt(m4[:, t], lg[:, t, 4:36].rearrange("p (g e) -> p g e", g=GROUPS),
                        hg[:, t, :].unsqueeze(2).to_broadcast([P, GROUPS, PER_GROUP]), ALU.mult))
            step.wait()
            e3 = e8[:, :].rearrange("p (t e) -> p t e", t=TT)
            for t in range(TT):
                step(dve.tensor_reduce(e3[:, t, :], m4[:, t].rearrange("p g e -> p e g"), AX, ALU.add))
            step.wait()
            first_max(e3, PER_GROUP, iota_e, best_1, hot_1[:, :])
            step(dve.scalar_tensor_tensor(e8[:, :], hot_1[:, :], -3.0e38, e8[:, :], ALU.mult, ALU.add))
            step.wait()
            first_max(e3, PER_GROUP, iota_e, best_2, hot_2[:, :])
            tt(diff, best_2, best_1, ALU.subtract).then_inc(exp_ok, 1)
            for t in range(TT):
                for mem, hot in ((mem0, hot_1), (mem1, hot_2)):
                    step(tt(mem[:, 32 * t:32 * t + 32].rearrange("p (g e) -> p g e", g=GROUPS),
                            hg[:, t, :].unsqueeze(2).to_broadcast([P, GROUPS, PER_GROUP]),
                            hot[:, 8 * t:8 * t + 8].unsqueeze(1).to_broadcast([P, GROUPS, PER_GROUP]), ALU.mult))
            step.wait()
            tt(mem_bf[:, :], mem0[:, :], mem1[:, :], ALU.add).then_inc(members_ok, 1)
            dve.wait_ge(exp_ok, 2)
            step(dve.tensor_reduce(red[:, :], exps.rearrange("p (t n) -> p t n", t=TT), AX, ALU.add))
            step.wait()
            step(dve.scalar_tensor_tensor(red[:, :], diff, 1.0, red[:, :], ALU.add, ALU.mult))
            step.wait()
            wt = wts[:, :].rearrange("p (t k) -> p t k", k=2)
            step(dve.reciprocal(wt[:, :, 0], red[:, :]))
            step.wait()
            step(tt(wt[:, :, 1], wt[:, :, 0], diff, ALU.mult))
            dve.wait_ge(ranked, 1)
            rank = bank[:, 7, 0:TT * 32]
            af = addr_f[:, :]
            m3 = masked[:, :].rearrange("p (t e) -> p t e", t=TT)
            me3 = masked_e[:, :].rearrange("p (t e) -> p t e", t=TT)
            exp_row = over_c[:, 0:32]
            slot = af[:, 0:8].rearrange("p (t k) -> p t k", k=2)
            eidx = af[:, 8:16].rearrange("p (t k) -> p t k", k=2)
            for k, mem in enumerate((mem0, mem1)):
                mm = mem[:, :].rearrange("p (t e) -> p t e", t=TT)
                step(tt(masked[:, :], mem[:, :], rank, ALU.mult))
                step(tt(me3, mm, exp_row.unsqueeze(1).to_broadcast([P, TT, 32]), ALU.mult))
                step.wait()
                step(dve.tensor_reduce(slot[:, :, k], m3, AX, ALU.add))
                step(dve.tensor_reduce(eidx[:, :, k], me3, AX, ALU.add))
                step.wait()
            blk = t32[:, 0:8]
            step(dve.tensor_scalar(blk, af[:, 0:8], float(P), None, ALU.is_ge))
            step.wait()
            for b in (2, 3):
                step(dve.scalar_tensor_tensor(blk, af[:, 0:8], float(b * P), blk, ALU.is_ge, ALU.add))
                step.wait()
            step(dve.scalar_tensor_tensor(t32[:, 8:16], af[:, 0:8], float(P), af[:, 8:16], ALU.mult, ALU.add))
            step.wait()
            step(dve.scalar_tensor_tensor(t32[:, 8:16], blk, float(32 - P * P), t32[:, 8:16], ALU.mult, ALU.add))
            step.wait()
            dve.tensor_scalar(addr[:, :], t32[:, 8:16], -float(EXPERTS), None, ALU.add).then_inc(addr_ok, 1)
            total = bank[:, 7, 128:160]
            for b in range(3):
                step(dve.tensor_scalar(over[:, 32 * b:32 * b + 32], total, float(P * (b + 1)), None, ALU.is_gt))
            step.wait()
            step(dve.memset(over_s[:, :], 0.0))
            step.wait()
            step(dve.tensor_tensor_scan(over_r[:, :], over[:, :], over_s[:, :], 0.0, ALU.add, ALU.add))
            step.wait()
            step(dve.tensor_copy(ovf_row[:, 16:17], over_r[:, 95:96]))
            step(tt(over_s[:, :], over_r[:, :], over[:, :], ALU.subtract))
            step.wait()
            step(dve.scalar_tensor_tensor(over_s[:, :], over_s[:, :], part[:, :], over[:, :], ALU.is_equal, ALU.mult))
            step.wait()
            step(tt(over_s[:, :], over_s[:, :], over_c[:, :], ALU.mult))
            step.wait()
            dve.tensor_reduce(ovf_col[:, :], over_s[:, :], AX, ALU.add).then_inc(ovf_ok, 1)
            dve.wait_ge(ovf_turned, 1)
            step(dve.tensor_copy(ovf_row[0:1, 0:8], bank[0:1, 7, 256:264]))
            step.wait()
            dve.tensor_scalar(ovf_row[0:1, 8:16], ovf_row[0:1, 0:8], 31, None, ALU.bitwise_and).then_inc(ovf_ready, 1)

            dve.wait_ge(lists_in, 16)
            dve.tensor_scalar(lists_x[:, :], lists[:, :], 1, None, ALU.logical_shift_right).then_inc(lists_x_ok, 1)

            def m_lo_part(u):
                dve.wait_ge(m_hi_ok, u.n + 1)
                sub(m_lo[:, u.slot % MSPLIT, :], m_raw[:, u.slot, :], m_hi[:, u.slot % MSPLIT, :]).then_inc(m_split_ok, 1)

            def xe_lo_part(s):
                dve.wait_ge(xe_hi_ok, s + 1)
                sub(xe_lo[:, :, :].rearrange("p (b k) n -> p b (k n)", b=2), bank[:, 4:6, :],
                    xe_hi[:, :, :].rearrange("p (b k) n -> p b (k n)", b=2)).then_inc(xe_split, 1)

            def ht_lo_part(s):
                dve.wait_ge(ht_hi_ok, s + 1)
                sub(ht_lo[:, :], bank[:, 6, :], ht_hi[:, :]).then_inc(ht_split, 1)

            def h_part(s, u):
                dve.wait_ge(m_done, u.n + 1 + MSPLIT)
                dve.wait_ge(m_silu, s + 1)
                tt(h_sb[:, :], bank[:, 1, :], silu[:, :], ALU.mult).then_inc(h_ok, 1)

            u = Unit(0, ring=MRING)
            m_lo_part(u)
            m_lo_part(u.ahead(1))
            xe_lo_part(0)
            for j in range(4):
                m_lo_part(u.ahead(j + 2))
            h_part(0, u.ahead(3))
            xe_lo_part(1)
            with dve.Fori(0, EXPERTS - 1) as i:
                u = Unit(4, 0, i, 6, MRING)
                m_lo_part(u.ahead(2))
                ht_lo_part(i)
                for j in range(3, 6):
                    m_lo_part(u.ahead(j))
                h_part(i + 1, u.ahead(3))
                m_lo_part(u.ahead(6))
                xe_lo_part(i + 2)
                m_lo_part(u.ahead(7))
            ht_lo_part(EXPERTS - 1)
            n_over = dve.value_load(ovf_row[0:1, 16:17], min_val=0, max_val=MAX_OVERFLOW)
            with dve.Fori(0, MAX_OVERFLOW) as j:
                with dve.If(n_over > j):
                    u = Unit(M_END, 0, j, 6, MRING)
                    xe_lo_part(j + (EXPERTS + 1))
                    for k in range(4):
                        m_lo_part(u.ahead(k))
                    h_part(j + EXPERTS, u.ahead(3))
                    ht_lo_part(j + EXPERTS)
                    m_lo_part(u.ahead(4))
                    m_lo_part(u.ahead(5))

            dve.wait_ge(x2a_ok, TT)
            dve.wait_ge(ln2_in, 32)
            for t in range(TT):
                dve.wait_ge(rows_in[t], 16)
                for k in range(2):
                    step(dve.scalar_tensor_tensor(x2[:, t, :], y_rows[:, t, D * k:D * k + D], wts[:, 2 * t + k:2 * t + k + 1],
                                                  x2[:, t, :], ALU.mult, ALU.add))
                    step.wait()
                layer_norm(t, ln2, f_var, f_std, f_ok)

        @block.tensor
        def _(pe):
            def products(dst, pairs, first=True, last=True):
                n = len(pairs)
                for x, (sh, sl, mh, ml) in enumerate(pairs):
                    pe.matmul(dst, sh, mh, start=first and x == 0, stop=False)
                    pe.matmul(dst, sh, ml, start=False, stop=False)
                    ins = pe.matmul(dst, sl, mh, start=False, stop=last and x == n - 1)
                return ins

            def ready(u):
                pe.wait_ge(split_done, u.n + 1 + RING)

            def cols_unit(u, b):
                ready(u)
                products(bank[:, b, :], [(w_hi[:, u.slot, P * k:P * k + P], w_lo[:, u.slot, P * k:P * k + P],
                                          xt_hi[:, k, :], xt_lo[:, k, :]) for k in range(KD)]).then_inc(units_done, 1)

            pe.sem_inc(units_done, RING)
            pe.sem_inc(rg_done, 6)
            pe.sem_inc(scored, 4)
            pe.sem_inc(pv_ok, 4)
            pe.sem_inc(turned, 4)
            pe.sem_inc(m_done, MSPLIT)
            pe.sem_inc(gates_ok, 6)
            pe.sem_inc(gelu_ok, 3)
            pe.sem_inc(normed_ok, 4)
            pe.sem_inc(y_ok, 1)
            pe.wait_ge(ident_ok, 2)
            pe.wait_ge(vec_in, 96)
            pe.transpose(bank[:, 7, 0:V_ROWS], vec_rows[0:V_ROWS, :], ident[0:V_ROWS, 0:V_ROWS]).then_inc(vec_turned, 1)
            for k in range(KD):
                for t in range(TT):
                    if k == 0:
                        pe.wait_ge(x_in[t], 16)
                    if k == 7 and t == 0:
                        pe.wait_ge(vec_ready, 1)
                    last = pe.transpose(bank[:, k, P * t:P * t + P], x_rows[:, t, P * k:P * k + P], ident[:, :])
                last.then_inc(xt_turned, 1)
            pe.wait_ge(xt_split, KD)

            def rg_tiles(s):
                pe.wait_ge(rg_split, s + 2)
                pe.wait_ge(conv_split, 3 * s + 3)
                where = {(0, 0): 0, (1, 0): 128, (0, 1): 256, (1, 1): 384, (2, 1): 512, (1, 2): 640, (2, 2): 768}
                for o, ins_t in enumerate(((0, 1), (0, 1, 2), (1, 2))):
                    for g, b in ((0, o), (1, (6, 7, 3)[o])):
                        if g == 0:
                            pe.wait_ge(u_out, 3 * s + o + 1)
                        elif o == 2:
                            pe.wait_ge(gelu_ok, 3 * s + 1 + 3)
                        pairs = [(rg_hi[:, g, where[o, t]:where[o, t] + P], rg_lo[:, g, where[o, t]:where[o, t] + P],
                                  conv_hi[:, t, :], conv_lo[:, t, :]) for t in ins_t]
                        products(bank[:, b, :], pairs).then_inc(rg_done, 1)

            with pe.Fori(0, 2) as i:
                for half in range(2):
                    s = 2 * i + half
                    for j in range(3):
                        pe.wait_ge(gates_ok, 6 * s + 2 * j + 1)
                        cols_unit(Unit(U_LRU, 6 * half + j, i, 12), j)
                    for j in range(3):
                        pe.wait_ge(gelu_ok, 3 * s + j + 1)
                        if j == 0:
                            pe.wait_ge(gates_ok, 6 * s + 6)
                        cols_unit(Unit(U_LRU, 6 * half + 3 + j, i, 12), 3 + j)
                    rg_tiles(s)
            for k in range(KD):
                if k < 2:
                    pe.wait_ge(gelu_ok, 12 + 3)
                else:
                    pe.wait_ge(grec_ok, k - 1)
                cols_unit(Unit(U_GREC, k), 4 + k % 2)
            pe.wait_ge(lru_split, WT + 3)
            pe.wait_ge(gates_ok, 24 + 6)
            with pe.Fori(0, 4) as i:
                for cc in range(2):
                    pe.wait_ge(lo_ok, 2 * i + cc + 1)
                    for j in range(2):
                        u = Unit(U_LO, 2 * cc + j, i, 4)
                        ready(u)
                        products(bank[:, cc, :], [(w_hi[:, u.slot, P * k:P * k + P], w_lo[:, u.slot, P * k:P * k + P],
                                                   lru_hi[:, 6 * j + k, :], lru_lo[:, 6 * j + k, :]) for k in range(6)],
                                 j == 0, j == 1).then_inc(units_done, 1)
            pe.wait_ge(lo_ok, 8 + 2)
            pe.wait_ge(grec_ok, KD)

            def pe_qk(h, u, ret=None):
                for j in range(4):
                    if j == 3 and ret is not None:
                        turn(ret)
                    pe.wait_ge(normed_ok, 4 * h + j + 1)
                    cols_unit(u.ahead(j), j)

            def turn(h):
                pe.wait_ge(normed_ok, 4 * h + 8)
                for j in range(4):
                    pe.wait_ge(silu_ok, 4 * h + j + 1)
                    for t in range(TT):
                        last = pe.transpose(bank[:, 4 + j, P * t:P * t + P], normed[:, t, P * j:P * j + P], ident[:, :])
                    last.then_inc(turned, 1)

            def pe_vg(h, u):
                for m in range(4):
                    ready(u.ahead(m))
                    slot = u.ahead(m).slot
                    for t in range(TT):
                        if m == 0:
                            pe.wait_ge(ret_out, 8 * h + 4 + t + 1)
                        last = products(bank[:, 4 + t, :], [
                            (xt_hi[:, 2 * m + k, P * t:P * t + P], xt_lo[:, 2 * m + k, P * t:P * t + P],
                             w_hi[:, slot, DV * k:DV * k + DV], w_lo[:, slot, DV * k:DV * k + DV]) for k in range(2)], m == 0, m == 3)
                    last.then_inc(units_done, 1)
                pe.wait_ge(qk_split, 4 * h + 4)
                for c_ in range(TT):
                    q0 = P * c_
                    products(bank[:, c_, 0:TOKENS - q0], [(qk_hi[:, 2 + k, q0:q0 + P], qk_lo[:, 2 + k, q0:q0 + P],
                                                          qk_hi[:, k, q0:TOKENS], qk_lo[:, k, q0:TOKENS]) for k in range(2)]).then_inc(scored, 1)
                for j in range(4):
                    pe.wait_ge(v_split, 4 * h + j + 1)
                    cols_unit(u.ahead(4 + j), 4 + j)
                spans = [0, 512, 896, 1152]
                for t in range(TT):
                    pe.wait_ge(p_split, 4 * h + t + 1)
                    products(bank[:, t, :], [(p_hi[:, spans[k] + P * (t - k):spans[k] + P * (t - k) + P],
                                              p_lo[:, spans[k] + P * (t - k):spans[k] + P * (t - k) + P],
                                              v_hi[:, k, :], v_lo[:, k, :]) for k in range(t + 1)]).then_inc(pv_ok, 1)

            def pe_ret(h, u):
                pe.wait_ge(ret_split, 4 * h + 8)
                for j in range(4):
                    ready(u.ahead(j))
                    slot = u.ahead(j).slot
                    for k in (2 * j, 2 * j + 1):
                        if k >= 4:
                            pe.wait_ge(ret_out, 8 * h + k - 3 + 8)
                        last = products(bank[:, 4 + k % 4, :], [
                            (w_hi[:, slot, 256 * x + P * (k % 2):256 * x + P * (k % 2) + P],
                             w_lo[:, slot, 256 * x + P * (k % 2):256 * x + P * (k % 2) + P],
                             ret_hi[:, x, :], ret_lo[:, x, :]) for x in range(4)])
                    last.then_inc(units_done, 1)

            pe_qk(0, Unit(U_QK0))
            with pe.Fori(0, HEADS - 1) as h:
                pe_vg(h, Unit(U_HEAD, 0, h, 16))
                pe_qk(h + 1, Unit(U_HEAD, 8, h, 16), h)
                pe_ret(h, Unit(U_HEAD, 12, h, 16))
            pe_vg(HEADS - 1, Unit(U_LAST))
            for k in range(KD):
                if k == 4:
                    turn(HEADS - 1)
                pe.wait_ge(normed_ok, 4 * HEADS + 4 if k >= 3 else 4 * HEADS + k + 1)
                if k >= 4:
                    pe.wait_ge(gret_ok, k - 3)
                cols_unit(Unit(U_GRET, k), k % 4)
            pe_ret(HEADS - 1, Unit(U_RET3))

            def turn_x2(t):
                pe.wait_ge(x2_ok, t + 1)
                if t:
                    pe.wait_ge(x2t_ok, t)
                for k in range(KD):
                    last = pe.transpose(bank[:, 4 + k // 4, P * (k % 4):P * (k % 4) + P], x2[:, t, P * k:P * k + P], ident[:, :])
                last.then_inc(x2_turned, 1)

            def router(t):
                pe.wait_ge(x2t_ok, t + 1)
                pe.wait_ge(router_in, 64)
                for k in range(KD):
                    last = pe.matmul(bank[:, 6, 36 * t:36 * t + 36], x2_t[:, t % 2, P * k:P * k + P], w_rt[:, 36 * k:36 * k + 36],
                                     start=k == 0, stop=k == KD - 1)
                last.then_inc(routed, 1)

            pe.wait_ge(split_done, U_END + RING)
            pe.wait_ge(gret_ok, KD)
            for t in range(TT):
                if t >= 2:
                    pe.wait_ge(z_ok, 2 * t - 2)
                for k in range(KD):
                    if t == 0:
                        pe.wait_ge(mrg_split, k + 1)
                    for half in range(2):
                        last = products(bank[:, 2 * (t % 2) + half, :], [
                            (mrg_hi[:, k, P * t:P * t + P], mrg_lo[:, k, P * t:P * t + P],
                             wo_hi[:, k, 512 * half:512 * half + 512], wo_lo[:, k, 512 * half:512 * half + 512])], k == 0, k == KD - 1)
                last.then_inc(proj_ok, 1)
                if t:
                    if t == 1:
                        pe.wait_ge(ret_out, 8 * HEADS + 8)
                    if t >= 2:
                        router(t - 2)
                    turn_x2(t - 1)
            router(TT - 2)
            turn_x2(TT - 1)
            router(TT - 1)
            pe.wait_ge(members_ok, 1)
            for t in range(TT + 1):
                dst = bank[:, 7, 32 * t:32 * t + 32]
                for k in range(min(t + 1, TT)):
                    last = pe.matmul(dst, tri_bf[:, :] if k == t else ones_bf[:, :], mem_bf[:, 32 * k:32 * k + 32],
                                     start=k == 0, stop=k == min(t, TT - 1))
            last.then_inc(ranked, 1)
            pe.wait_ge(ovf_ok, 1)
            pe.transpose(bank[0:1, 7, 256:256 + P], ovf_col[:, :], ident[:, :]).then_inc(ovf_turned, 1)

            def turn_x(s, ahead=0):
                pe.wait_ge(xg_in, 16 * s + 16 * (1 + ahead))
                if not (isinstance(s, int) and s == 0):
                    pe.wait_ge(xe_split, s)
                for k in range(KD):
                    last = pe.transpose(bank[:, 4 + k // 4, P * (k % 4):P * (k % 4) + P], xg[:, P * k:P * k + P], ident[:, :])
                last.then_inc(xe_turned, 1)

            def gate_up(s, u):
                pe.wait_ge(xe_split, s + 1)
                for b in range(2):
                    for half in range(2):
                        v = u.ahead(2 * b + half)
                        pe.wait_ge(m_split_ok, v.n + 1 + MRING)
                        sl = v.slot % MSPLIT
                        products(bank[:, b, :], [(xe_hi[:, 4 * half + k, :], xe_lo[:, 4 * half + k, :],
                                                  m_hi[:, sl, FE * k:FE * k + FE], m_lo[:, sl, FE * k:FE * k + FE]) for k in range(4)],
                                 half == 0, half == 1).then_inc(m_done, 1)

            def turn_h(s):
                pe.wait_ge(h_ok, s + 1)
                for k in range(4):
                    last = pe.transpose(bank[:, 6, P * k:P * k + P], h_sb[:, P * k:P * k + P], ident[:, :])
                last.then_inc(h_turned, 1)

            def down(s, u):
                pe.wait_ge(ht_split, s + 1)
                pe.wait_ge(y_ok, s + 1)
                for half in range(2):
                    v = u.ahead(half)
                    pe.wait_ge(m_split_ok, v.n + 1 + MRING)
                    sl = v.slot % MSPLIT
                    for b in range(2):
                        last = products(bank[:, 2 + b, :], [
                            (ht_hi[:, P * (2 * half + k):P * (2 * half + k) + P], ht_lo[:, P * (2 * half + k):P * (2 * half + k) + P],
                             m_hi[:, sl, 1024 * k + 512 * b:1024 * k + 512 * b + 512], m_lo[:, sl, 1024 * k + 512 * b:1024 * k + 512 * b + 512])
                            for k in range(2)], half == 0, half == 1)
                    last.then_inc(m_done, 1)

            turn_x(0)
            gate_up(0, Unit(0, ring=MRING))
            turn_x(1)
            turn_h(0)
            with pe.Fori(0, EXPERTS - 1) as i:
                u = Unit(4, 0, i, 6, MRING)
                gate_up(i + 1, u)
                turn_x(i + 2)
                down(i, u.ahead(4))
                turn_h(i + 1)
            down(EXPERTS - 1, Unit(M_LAST, ring=MRING))
            pe.wait_ge(ovf_ready, 1)
            n_over = pe.value_load(ovf_row[0:1, 16:17], min_val=0, max_val=MAX_OVERFLOW)
            with pe.Fori(0, MAX_OVERFLOW) as j:
                with pe.If(n_over > j):
                    u = Unit(M_END, 0, j, 6, MRING)
                    turn_x(j + (EXPERTS + 1), 1)
                    gate_up(j + EXPERTS + 1, u)
                    turn_h(j + EXPERTS)
                    down(j + EXPERTS, u.ahead(4))


_INS = ['x', 'w_in', 'b_merge', 'conv_w', 'conv_b', 'w_rg_r', 'b_rg_r', 'w_rg_i', 'b_rg_i', 'lru_lambda', 'w_ret_o',
        'w_lru_o', 'w_out', 'ln1_g', 'ln1_b', 'w_group', 'b_group', 'w_exp_router', 'b_exp_router', 'w_e_gate',
        'w_e_up', 'w_e_down', 'ln2_g', 'ln2_b']


def _tables():
    half = DK // 2
    inv = np.float32(10000.0) ** (-np.arange(half, dtype=np.float32) / np.float32(half))
    ang = np.arange(TOKENS, dtype=np.float32)[None, :] * inv[:, None]
    rope = np.stack([np.cos(ang), np.sin(ang)]).astype(np.float32)
    log_g = np.log1p(-(2.0 ** (-5.0 - np.arange(HEADS))))
    diff = np.arange(TOKENS)[None, :] - np.arange(P)[:, None]
    decay = np.where(diff >= 0, np.exp(log_g[:, None, None] * np.maximum(diff, 0)), 0.0) * DK ** -0.5
    return rope, decay.astype(np.float32)


def kernel(**inputs):
    import concourse.bacc as _bacc
    from concourse.bass_utils import run_bass_kernel_spmd as _run

    nc = _bacc.Bacc("TRN2", target_bir_lowering=False, num_devices=1)
    arrays, io = {}, {}
    rope, decay = _tables()
    given = {n: inputs[n] for n in _INS}
    given.update(rope=rope, decay=decay)
    for name, value in given.items():
        a = np.ascontiguousarray(value)
        arrays[f"in_{name}_dram"] = a
        io[name] = nc.dram_tensor(f"in_{name}_dram", a.shape, mybir.dt.from_np(a.dtype), kind="ExternalInput").ap()
    out = nc.dram_tensor("out_0_dram", (1, TOKENS, D), F32, kind="ExternalOutput").ap()
    layer(nc, io, out)
    r = _run(nc, [arrays], core_ids=[0])
    return r.results[0]["out_0_dram"]
```

```python
from contextlib import ExitStack

import numpy as np

import concourse.bass as bass
from concourse import mybir

F32 = mybir.dt.float32
F32R = mybir.dt.float32r
BF16 = mybir.dt.bfloat16
I32 = mybir.dt.int32
ALU = mybir.AluOpType
ACT = mybir.ActivationFunctionType
AX = mybir.AxisListType.X
ds = bass.ds

P = 128
TOKENS, D = 512, 1024
TT = TOKENS // P
KD = D // P
HEADS, DK, DV = 4, 256, 512
WIDTH, BLOCK = 1536, 192
WT = WIDTH // P
GROUPS, PER_GROUP, EXPERTS, FE = 4, 8, 32, 512
OFF_Q, OFF_K, OFF_V = 0, HEADS * DK, 2 * HEADS * DK
OFF_G = OFF_V + HEADS * DV
OFF_U = OFF_G + HEADS * DV
OFF_GATE = OFF_U + WIDTH
OFF_MERGE = OFF_GATE + WIDTH
EPS = 1e-5
ALPHA = 2.0 ** 0.25
ROWS = 64
BLOCKS = TOKENS // ROWS
MAX_OVERFLOW = (2 * TOKENS) // ROWS - 1
LIST_COLS = BLOCKS * EXPERTS
OVER = (BLOCKS - 1) * EXPERTS
NO_ROW = 4096

V_CONV_W, V_CONV_B, V_BR, V_BI, V_LAM, V_MERGE, V_ROWS = 0, 48, 60, 72, 84, 96, 112

RING = 4
U_LRU = 0
U_GREC = U_LRU + 24
U_LO = U_GREC + 8
U_QK0 = U_LO + 16
U_HEAD = U_QK0 + 4
U_LAST = U_HEAD + 48
U_GRET = U_LAST + 8
U_RET3 = U_GRET + 8
U_OUT = U_RET3 + 4
U_END = U_OUT + 8

MRING, MSPLIT = 12, 3
PAIRS = (EXPERTS - 1) // 2
M_LAST = 4 + 6 * (EXPERTS - 1)
M_END = M_LAST + 2


class Unit:

    def __init__(self, base, j=0, i=0, per=0, ring=RING):
        assert per % ring == 0
        self.at = (base, i, per, ring)
        self.n = base + j + per * i
        self.j = j
        self.slot = (base + j) % ring
        self.fill = (base + j) // ring + (per // ring) * i + 1

    def ahead(self, d):
        base, i, per, ring = self.at
        return Unit(base, self.j + d, i, per, ring)


class Steps:

    def __init__(self, eng, sem):
        self.eng, self.sem, self.done, self.more = eng, sem, 0, 0

    def __call__(self, ins):
        ins.then_inc(self.sem, 1)
        self.done += 1

    def wait(self):
        self.eng.wait_ge(self.sem, self.done + self.more)

    def enter(self, i, per):
        self.more, self.start, self.per = i * per, self.done, per

    def leave(self, times):
        assert self.done - self.start == self.per, (self.done - self.start, self.per)
        self.more, self.done = 0, self.start + self.per * times


def layer(nc, io, out):
    ctx = ExitStack()
    with ctx:
        BASE = 16896
        ctx.enter_context(nc.sbuf_tensor("fence", [P, 53000], F32))

        def at(name, kb, shape, dt=F32):
            return nc.alloc_sbuf_tensor_at(name, shape, dt, offset=BASE + int(kb * 1024))

        def sem(name):
            return ctx.enter_context(nc.semaphore(name))

        bank = ctx.enter_context(nc.psum_tensor("bank", [P, 8, 512], F32))

        xt_hi, xt_lo = at("xt_hi", 0, [P, KD, TOKENS], F32R), at("xt_lo", 16, [P, KD, TOKENS], F32R)
        raw = at("raw", 32, [P, RING, 1024])
        w_hi, w_lo = at("w_hi", 48, [P, RING, 1024], F32R), at("w_lo", 64, [P, RING, 1024], F32R)
        merge = at("merge", 80, [P, KD, TOKENS])
        x_rows = at("x_rows", 144, [P, TT, D])
        vec_rows = at("vec_rows", 160, [P, P])
        rg_raw, rg_hi = at("rg_raw", 80, [P, 2, 896]), at("rg_hi", 87, [P, 2, 896], F32R)
        rg_lo = at("rg_lo", 197, [P, 2, 896], F32R)
        lru_hi, lru_lo = at("lru_hi", 96, [P, WT, TOKENS], F32R), at("lru_lo", 120, [P, WT, TOKENS], F32R)
        u_ext = at("u_ext", 144, [P, 3, TOKENS + 4])
        conv = at("conv", 151, [P, 3, TOKENS])
        conv_hi, conv_lo = at("conv_hi", 157, [P, 3, TOKENS], F32R), at("conv_lo", 163, [P, 3, TOKENS], F32R)
        gelu = at("gelu", 169, [P, 3, TOKENS])
        r_t, i_t, s_t = at("r_t", 175, [P, 3, TOKENS]), at("i_t", 181, [P, 3, TOKENS]), at("s_t", 187, [P, 3, TOKENS])
        inv = at("inv", 193, [P, TOKENS])
        acc = at("acc", 96, [P, KD, TOKENS])
        p_hi, p_lo, p_f = at("p_hi", 112, [P, 1280], F32R), at("p_lo", 117, [P, 1280], F32R), at("p_f", 122, [P, 1280])
        ret_hi, ret_lo = at("ret_hi", 112, [P, 4, TOKENS], F32R), at("ret_lo", 120, [P, 4, TOKENS], F32R)
        qk_hi, qk_lo = at("qk_hi", 128, [P, 4, TOKENS], F32R), at("qk_lo", 136, [P, 4, TOKENS], F32R)
        v_hi, v_lo = at("v_hi", 144, [P, TT, DV], F32R), at("v_lo", 152, [P, TT, DV], F32R)
        normed = at("normed", 160, [P, TT, DV])
        gated = at("gated", 168, [P, 4, TOKENS])
        rope = at("rope", 176, [P, 2, TOKENS])
        decay = at("decay", 180, [P, HEADS, TOKENS])
        rope_a, rope_b = at("rope_a", 188, [P, TOKENS]), at("rope_b", 190, [P, TOKENS])
        rope_o = at("rope_o", 192, [P, 4, TOKENS])
        g_ret = at("g_ret", 176, [P, KD, TOKENS])
        mrg_hi, mrg_lo = at("mrg_hi", 160, [P, KD, TOKENS], F32R), at("mrg_lo", 176, [P, KD, TOKENS], F32R)
        wo_hi, wo_lo = at("wo_hi", 0, [P, KD, D], F32R), at("wo_lo", 128, [P, KD, D], F32R)
        ln1 = at("ln1", 32, [P, 2, D])
        x_res = at("x_res", 48, [P, TT, D])
        x2 = at("x2", 64, [P, TT, D])
        x2_t = at("x2_t", 192, [P, 2, D])
        m_hi, m_lo = at("m_hi", 0, [P, MSPLIT, 2048], F32R), at("m_lo", 24, [P, MSPLIT, 2048], F32R)
        m_raw = [at(f"m_raw{n}", kb, [P, 2048]) for n, kb in enumerate((80, 88, 96, 104, 112, 120, 176, 184, 48, 56, 152, 192))]
        xe_hi, xe_lo = at("xe_hi", 128, [P, KD, P], F32R), at("xe_lo", 132, [P, KD, P], F32R)
        xg = at("xg", 136, [P, D])
        y_sb = at("y_sb", 140, [P, D])
        silu, h_sb = at("silu", 144, [P, FE]), at("h_sb", 146, [P, FE])
        ht_hi, ht_lo = at("ht_hi", 148, [P, FE // P, P], F32R), at("ht_lo", 150, [P, FE // P, P], F32R)
        bank_x = bank[:, 4:6, :].rearrange("p b (k n) -> p (b k) n", n=P)
        bank_h = bank[:, 6, :].rearrange("p (k n) -> p k n", n=P)
        ln2 = at("ln2", 160, [P, 2, D])
        y_rows = at("y_rows", 80, [P, TT, 2 * D])
        c = [204.25]

        def small(name, cols, dt=F32, size=4):
            t = at(name, c[0], [P, cols], dt)
            c[0] += (cols * size + 31) // 32 * 32 / 1024
            return t

        ident = small("ident", P)
        vec = small("vec", V_ROWS)
        rate = small("rate", WT)
        cur = small("cur", 2 * 7 * 3)
        cur_v = cur[:, :].rearrange("p (b k j) -> p b k j", b=2, k=7)
        stats, mv = small("stats", 12), small("mv", 2)
        scale_v = small("scale_v", 3)
        wts = small("wts", 8)
        lists = small("lists", LIST_COLS, I32)
        cur_rate = small("cur_rate", 12)
        x_idx, y_idx = small("x_idx", 1, I32), small("y_idx", 1, I32)
        ovf_row = small("ovf_row", 2 * 16 + 1, I32)
        assert c[0] <= 207.4, c[0]
        rt_kb = [200.0]

        def rt(name, shape, dt=F32, size=4):
            t = at(name, rt_kb[0], [P, shape], dt)
            rt_kb[0] += (shape * size + 31) // 32 * 32 / 1024
            return t

        logit = rt("logit", TT * 36)
        w_rt = rt("w_rt", KD * 36)
        b_rt = rt("b_rt", 36)
        iota_g, iota_e = rt("iota_g", 4), rt("iota_e", 8)
        hot_g, hot_1, hot_2, e8 = rt("hot_g", 16), rt("hot_1", 32), rt("hot_2", 32), rt("e8", 32)
        slot_i, red, res = rt("slot_i", 32, I32), rt("red", 4), rt("res", 64)
        val = rt("val", 8, I32)
        assert rt_kb[0] <= 204.25
        ones_bf, tri_bf = at("ones_bf", 173, [P, P], BF16), at("tri_bf", 173.25, [P, P], BF16)
        masked, masked_e = at("masked", 173.5, [P, TT * 32]), at("masked_e", 174, [P, TT * 32])
        mem0, mem1 = at("mem0", 174.5, [P, TT * 32]), at("mem1", 175, [P, TT * 32])
        mem_bf = at("mem_bf", 175.5, [P, TT * 32], BF16)
        lists_x = at("lists_x", 172, [P, LIST_COLS], I32)
        over, over_r = at("over", 168, [P, OVER]), at("over_r", 169, [P, OVER])
        over_s, over_c = at("over_s", 170, [P, OVER]), at("over_c", 171, [P, OVER])
        ovf_col, part = at("ovf_col", 168.875, [P, 1]), at("part", 168.9375, [P, 1])
        addr = at("addr", 169.875, [P, 8], I32)
        addr_f = at("addr_f", 170.875, [P, 16])

        x2_dram = nc.dram_tensor("x2_dram", [TOKENS, D], F32).ap()
        y_dram = nc.dram_tensor("y_dram", [2 * TOKENS, D], F32).ap()
        list_dram = nc.dram_tensor("list_dram", [ROWS * LIST_COLS, 1], I32).ap()

        loaded = [sem(f"weights_loaded{k}") for k in range(RING)]
        hi_done, split_done, units_done = sem("hi_done"), sem("split_done"), sem("units_done")
        vec_in, x_in, vec_turned, vec_ready = sem("vec_in"), [sem(f"x_in{t}") for t in range(TT)], sem("vec_turned"), sem("vec_ready")
        ident_ok, xt_turned, xt_hi_ok, xt_split = sem("ident_ok"), sem("xt_turned"), sem("xt_hi_ok"), sem("xt_split")
        lam_e, rate_ok, pads_ok = sem("lam_e"), sem("rate_ok"), sem("pads_ok")
        rg_in, rg_hi_ok, rg_split, rg_done = sem("rg_in"), sem("rg_hi_ok"), sem("rg_split"), sem("rg_done")
        cur_ok, u_out, conv_ok, conv_hi_ok, conv_split = sem("cur_ok"), sem("u_out"), sem("conv_ok"), sem("conv_hi_ok"), sem("conv_split")
        gelu_ok, gates_ok, tanh_ok, decay_ok, sqrt_ok, tail_ok, lru_split = sem("gelu_ok"), sem("gates_ok"), sem("tanh_ok"), sem("decay_ok"), sem("sqrt_ok"), sem("tail_ok"), sem("lru_split")
        grec_ok, lo_ok = sem("grec_ok"), sem("lo_ok")
        tables_in = sem("tables_in")
        roped, qk_hi_ok, qk_split = sem("roped"), sem("qk_hi_ok"), sem("qk_split")
        v_hi_ok, v_split = sem("v_hi_ok"), sem("v_split")
        scored, masked_ok, p_hi_ok, p_split, pv_ok = sem("scored"), sem("masked_ok"), sem("p_hi_ok"), sem("p_split"), sem("pv_ok")
        silu_ok, var_ok, std_ok, rstd_ok, normed_ok = sem("silu_ok"), sem("var_ok"), sem("std_ok"), sem("rstd_ok"), sem("normed_ok")
        turned, retf_ok, ret_hi_ok, ret_split, ret_out = sem("turned"), sem("retf_ok"), sem("ret_hi_ok"), sem("ret_split"), sem("ret_out")
        gret_ok, acc_ok, merged, mrg_hi_ok, mrg_split = sem("gret_ok"), sem("acc_ok"), sem("merged"), sem("mrg_hi_ok"), sem("mrg_split")
        ln1_in, res_in = sem("ln1_in"), sem("res_in")
        proj_ok, z_ok, x2_var, x2_std, x2_ok = (sem(n) for n in ("proj_ok", "z_ok", "x2_var", "x2_std", "x2_ok"))
        x2_turned, x2t_ok, routed, x2_stored = sem("x2_turned"), sem("x2t_ok"), sem("routed"), sem("x2_stored")
        router_in, consts_ok = sem("router_in"), sem("consts_ok")
        dve_steps, pool_steps = sem("dve_steps"), sem("pool_steps")
        list_empty, exp_ok, members_ok, ranked, ovf_ok, ovf_turned, addr_ok = (sem(n) for n in ("list_empty", "exp_ok", "members_ok", "ranked", "ovf_ok", "ovf_turned", "addr_ok"))
        list_set, scattered, lists_in, idx_ok, ovf_ready, x2a_ok = (sem(n) for n in ("list_set", "scattered", "lists_in", "idx_ok", "ovf_ready", "x2a_ok"))
        m_loaded = [sem(f"m_loaded{k}") for k in range(MRING)]
        m_hi_ok, m_split_ok, m_done = sem("m_hi_ok"), sem("m_split_ok"), sem("m_done")
        xg_in, xe_turned, xe_hi_ok, xe_split = sem("xg_in"), sem("xe_turned"), sem("xe_hi_ok"), sem("xe_split")
        m_silu, h_ok, h_turned, ht_hi_ok, ht_split = sem("m_silu"), sem("h_ok"), sem("h_turned"), sem("ht_hi_ok"), sem("ht_split")
        y_ok, y_sent, y_free, marks, lists_x_ok = sem("y_ok"), sem("y_sent"), sem("y_free"), sem("marks"), sem("lists_x_ok")
        moe_done, rows_in, ln2_in = sem("moe_done"), [sem(f"rows_in{t}") for t in range(TT)], sem("ln2_in")
        f_var, f_std, f_ok, stored, first_scaled, first_ok = (sem(n) for n in ("f_var", "f_std", "f_ok", "stored", "first_scaled", "first_ok"))

        w_in = io["w_in"][0].rearrange("(k p) n -> p k n", p=P)
        w_lru = io["w_lru_o"][0].rearrange("(k p) n -> p k n", p=P)
        w_ret = io["w_ret_o"][0].rearrange("(k p) n -> p k n", p=P)
        w_out = io["w_out"][0].rearrange("(k p) n -> k p n", p=P)
        w_gate = io["w_e_gate"][0].rearrange("e (k p) n -> p e k n", p=P)
        w_up = io["w_e_up"][0].rearrange("e (k p) n -> p e k n", p=P)
        w_down = io["w_e_down"][0].rearrange("e (k p) n -> p e k n", p=P)
        x_view = io["x"][0].rearrange("(t p) d -> t p d", p=P)
        out_view = out[0].rearrange("(t p) d -> t p d", p=P)

        def row(v):
            return v.rearrange("a n -> (a n)").partition_broadcast(P)

        block = ctx.enter_context(nc.Block())

        @block.sync
        def _(sp):
            def load(u, dst_cols, src, k):
                sp.wait_ge(split_done, u.n + 1)
                dst = raw[:, u.slot, 0:dst_cols].rearrange("p (k n) -> p k n", k=k)
                sp.dma_start(dst, src).then_inc(loaded[u.slot], 16)

            def load_cols(u, col):
                load(u, 1024, w_in[:, :, ds(col, P)] if not isinstance(col, int) else w_in[:, :, col:col + P], KD)

            vectors = [("conv_w", V_CONV_W, 48), ("conv_b", V_CONV_B, 12), ("b_rg_r", V_BR, 12),
                       ("b_rg_i", V_BI, 12), ("lru_lambda", V_LAM, 12), ("b_merge", V_MERGE, 16)]
            for name, r, n in vectors:
                src = io[name][0]
                src = src.rearrange("k (t p) -> (k t) p", p=P) if name == "conv_w" else src.rearrange("(t p) -> t p", p=P)
                sp.dma_start(vec_rows[r:r + n, :], src).then_inc(vec_in, 16)

            def load_gates(s):
                sp.wait_ge(rg_split, s + 1)
                for g, w in enumerate((io["w_rg_r"][0], io["w_rg_i"][0])):
                    a = w[ds(2 * s, 1)].rearrange("a i o -> (a i) o")
                    b = w[ds(2 * s + 1, 1)].rearrange("a i o -> (a i) o")
                    sp.dma_start(rg_raw[:, g, 0:192], a[0:128, :]).then_inc(rg_in, 16)
                    sp.dma_start(rg_raw[0:64, g, 256:448], a[128:192, :]).then_inc(rg_in, 16)
                    sp.dma_start(rg_raw[64:128, g, 448:640], b[0:64, :]).then_inc(rg_in, 16)
                    sp.dma_start(rg_raw[:, g, 704:896], b[64:192, :]).then_inc(rg_in, 16)

            sp.wait_ge(pads_ok, 1)
            with sp.Fori(0, 2) as i:
                for half in range(2):
                    s = 2 * i + half
                    for j in range(3):
                        load_cols(Unit(U_LRU, 6 * half + j, i, 12), s * 384 + (OFF_U + P * j))
                    for j in range(3):
                        if j == 2:
                            load_gates(s)
                        load_cols(Unit(U_LRU, 6 * half + 3 + j, i, 12), s * 384 + (OFF_GATE + P * j))
            for k in range(KD):
                load_cols(Unit(U_GREC, k), OFF_MERGE + D + P * k)
            with sp.Fori(0, 4) as i:
                for cc in range(2):
                    for part_k in range(2):
                        load(Unit(U_LO, 2 * cc + part_k, i, 4), 768, w_lru[:, 6 * part_k:6 * part_k + 6, ds(i * 256 + cc * P, P)], 6)

            def load_qk(h, u):
                for j in range(4):
                    load_cols(u.ahead(j), h * DK + (OFF_Q + P * j if j < 2 else OFF_K + P * (j - 2)))

            def load_vg(h, u):
                for j in range(4):
                    load(u.ahead(j), 1024, w_in[:, 2 * j:2 * j + 2, ds(h * DV + OFF_V, DV)] if not isinstance(h, int)
                         else w_in[:, 2 * j:2 * j + 2, OFF_V + h * DV:OFF_V + h * DV + DV], 2)
                for j in range(4):
                    load_cols(u.ahead(4 + j), h * DV + (OFF_G + P * j))

            def load_ret(h, u):
                for j in range(4):
                    rows = w_ret[:, ds(4 * h, 4), 256 * j:256 * j + 256] if not isinstance(h, int) else w_ret[:, 4 * h:4 * h + 4, 256 * j:256 * j + 256]
                    load(u.ahead(j), 1024, rows, 4)

            sp.wait_ge(lru_split, WT + 3)
            sp.wait_ge(conv_split, WT)
            sp.dma_start(rope[:, :, :], io["rope"].rearrange("a p n -> p a n")).then_inc(tables_in, 16)
            sp.dma_start(decay[:, :, :], io["decay"].rearrange("h p n -> p h n")).then_inc(tables_in, 16)
            sp.wait_ge(rg_done, 24 + 6)
            w_rt_v = w_rt[:, :].rearrange("p (k n) -> p k n", k=KD)
            sp.dma_start(w_rt_v[:, :, 0:GROUPS], io["w_group"][0].rearrange("(k p) n -> p k n", p=P)).then_inc(router_in, 16)
            sp.dma_start(w_rt_v[:, :, GROUPS:36], io["w_exp_router"][0].rearrange("(k p) n -> p k n", p=P)).then_inc(router_in, 16)
            sp.dma_start(b_rt[:, 0:GROUPS], row(io["b_group"])).then_inc(router_in, 16)
            sp.dma_start(b_rt[:, GROUPS:36], row(io["b_exp_router"])).then_inc(router_in, 16)
            load_qk(0, Unit(U_QK0))
            with sp.Fori(0, HEADS - 1) as h:
                load_vg(h, Unit(U_HEAD, 0, h, 16))
                load_qk(h + 1, Unit(U_HEAD, 8, h, 16))
                load_ret(h, Unit(U_HEAD, 12, h, 16))
            load_vg(HEADS - 1, Unit(U_LAST))
            for k in range(KD):
                load_cols(Unit(U_GRET, k), OFF_MERGE + P * k)
            load_ret(HEADS - 1, Unit(U_RET3))
            for k in range(KD):
                u = Unit(U_OUT, k)
                sp.wait_ge(split_done, u.n + 1)
                sp.dma_start(raw[:, u.slot, :], w_out[k]).then_inc(loaded[u.slot], 16)

            sp.wait_ge(split_done, U_END + RING)
            sp.wait_ge(units_done, U_OUT + RING)
            sp.dma_start(ln1[:, 0, :], row(io["ln1_g"])).then_inc(ln1_in, 16)
            sp.dma_start(ln1[:, 1, :], row(io["ln1_b"])).then_inc(ln1_in, 16)
            sp.dma_start(x_res[:, :, :], io["x"][0].rearrange("(t p) d -> p t d", p=P)).then_inc(res_in, 16)

            sp.wait_ge(mrg_split, KD)

            def load_m(u, src):
                sp.wait_ge(m_split_ok, u.n + 1)
                k = 4 if src.shape[-1] == FE else 2
                sp.dma_start(m_raw[u.slot][:, :].rearrange("p (k n) -> p k n", k=k), src).then_inc(m_loaded[u.slot], 16)

            def expert(w, e, k0, k1):
                return w[:, ds(e, 1), k0:k1, :].rearrange("p e k n -> p (e k) n")

            def load_half(w, e, u):
                for half in range(2):
                    load_m(u.ahead(half), expert(w, e, 4 * half, 4 * half + 4))

            def load_gate_up(e, u):
                load_half(w_gate, e, u)
                load_half(w_up, e, u.ahead(2))

            def load_down(e, u):
                for half in range(2):
                    load_m(u.ahead(half), expert(w_down, e, 2 * half, 2 * half + 2))

            load_gate_up(0, Unit(0, ring=MRING))
            load_half(w_gate, 1, Unit(4, ring=MRING))
            def store_x2(t):
                sp.wait_ge(x2_ok, t + 1)
                sp.dma_start(x2_dram[t * P:(t + 1) * P, :], x2[:, t, :]).then_inc(x2_stored, 16)

            for t in range(TT - 2):
                store_x2(t)
            sp.wait_ge(proj_ok, TT)
            load_half(w_up, 1, Unit(6, ring=MRING))
            store_x2(TT - 2)
            sp.wait_ge(z_ok, 2 * TT)
            load_down(0, Unit(8, ring=MRING))
            store_x2(TT - 1)
            sp.wait_ge(routed, TT)
            load_half(w_gate, 2, Unit(10, ring=MRING))
            sp.dma_start(ln2[:, 0, :], row(io["ln2_g"])).then_inc(ln2_in, 16)
            sp.dma_start(ln2[:, 1, :], row(io["ln2_b"])).then_inc(ln2_in, 16)
            sp.wait_ge(scattered, 16 * 8)
            sp.dma_start(lists[0:ROWS, :], list_dram.rearrange("(p n) a -> p (n a)", p=ROWS)).then_inc(lists_in, 16)

            def load_next(e, u):
                load_half(w_up, e + 1, u)
                load_down(e, u.ahead(2))
                load_half(w_gate, e + 2, u.ahead(4))

            with sp.Fori(0, PAIRS - 1) as i:
                for b in range(2):
                    load_next(2 * i + (1 + b), Unit(12 + 6 * b, 0, i, 12, MRING))
            load_next(EXPERTS - 3, Unit(M_LAST - 10, ring=MRING))
            load_half(w_up, EXPERTS - 1, Unit(M_LAST - 4, ring=MRING))
            load_down(EXPERTS - 2, Unit(M_LAST - 2, ring=MRING))
            load_down(EXPERTS - 1, Unit(M_LAST, ring=MRING))
            sp.wait_ge(ovf_ready, 1)
            n_over = sp.value_load(ovf_row[0:1, 32:33], min_val=0, max_val=MAX_OVERFLOW)
            with sp.If(n_over > 0):
                with sp.Fori(0, (MAX_OVERFLOW + 1) // 2) as i:
                    for b in range(2):
                        j = 2 * i + b
                        with sp.If(n_over > j):
                            e = sp.value_load(ovf_row[0:1, ds(j + 16, 1)], min_val=0, max_val=EXPERTS - 1)
                            load_gate_up(e, Unit(M_END + 6 * b, 0, i, 12, MRING))
                            load_down(e, Unit(M_END + 6 * b, 4, i, 12, MRING))
            sp.wait_ge(moe_done, 1)
            for t in range(TT):
                sp.dma_start(y_rows[:, t, :], y_dram[2 * P * t:2 * P * (t + 1), :].rearrange("(p k) d -> p (k d)", k=2)).then_inc(rows_in[t], 16)
            for t in range(TT):
                sp.wait_ge(f_ok, t + 1)
                sp.dma_start(out_view[t], x2[:, t, :]).then_inc(stored, 16)
            sp.wait_ge(stored, 16 * TT)

        @block.gpsimd
        def _(pool):
            steps = Steps(pool, pool_steps)
            pool.memset(ident[:, :], 0.0).then_inc(ident_ok, 1)
            pool.wait_ge(ident_ok, 1)
            pool.affine_select(out=ident[:, :], in_=ident[:, :], compare_op=ALU.not_equal, fill=1.0, base=0,
                               pattern=[[-1, P]], channel_multiplier=1).then_inc(ident_ok, 1)
            pool.memset(rg_raw[:, :, :], 0.0).then_inc(pads_ok, 1)
            pool.memset(lists[:, :], NO_ROW).then_inc(list_set, 1)
            pool.wait_ge(list_set, 1)
            pool.dma_start(list_dram.rearrange("(p n) a -> p (n a)", p=P), lists[:, 0:ROWS * LIST_COLS // P]).then_inc(list_empty, 16)
            pool.wait_ge(ret_out, 8 * HEADS)
            for k in range(KD):
                pool.wait_ge(gret_ok, k + 1)
                steps(pool.tensor_tensor(acc[:, k, :], acc[:, k, :], g_ret[:, k, :], ALU.mult))
                steps.wait()
                pool.tensor_tensor(acc[:, k, :], acc[:, k, :], merge[:, k, :], ALU.add).then_inc(acc_ok, 1)
            pool.wait_ge(proj_ok, TT)
            pool.iota(iota_g[:, :], pattern=[[1, 4]], base=-4, channel_multiplier=0, allow_small_or_imprecise_dtypes=True)
            pool.iota(iota_e[:, :], pattern=[[1, 8]], base=-8, channel_multiplier=0, allow_small_or_imprecise_dtypes=True)
            pool.iota(part[:, :], pattern=[[1, 1]], base=0, channel_multiplier=1, allow_small_or_imprecise_dtypes=True)
            pool.iota(over_c[:, :], pattern=[[1, OVER]], base=EXPERTS, channel_multiplier=0, allow_small_or_imprecise_dtypes=True)
            pool.iota(val[:, :], pattern=[[2 * P, TT], [1, 2]], base=0, channel_multiplier=2)
            pool.memset(xg[:, :], 0.0)
            pool.memset(ones_bf[:, :], 1.0).then_inc(pads_ok, 1)
            pool.wait_ge(pads_ok, 2)
            pool.affine_select(out=tri_bf[:, :], in_=ones_bf[:, :], compare_op=ALU.is_gt, fill=0.0, base=0,
                               pattern=[[1, P]], channel_multiplier=-1).then_inc(consts_ok, 1)
            last_x, last_y = pool.to_reg(TOKENS - 1), pool.to_reg(2 * TOKENS - 1)
            pool.wait_ge(list_empty, 16)
            pool.wait_ge(addr_ok, 1)
            for n in range(8):
                pool.indirect_dma_start(list_dram, bass.IndirectOffsetOnAxis(ap=addr[:, n:n + 1], axis=0), val[:, n:n + 1], None).then_inc(scattered, 16)

            def gather(col):
                steps(pool.tensor_copy(x_idx[0:ROWS, :], lists_x[0:ROWS, ds(col, 1)] if not isinstance(col, int) else lists_x[0:ROWS, col:col + 1]))
                steps.wait()
                pool.sem_inc(marks, 1)
                pool.indirect_dma_start(xg[0:ROWS, :], None, x2_dram, bass.IndirectOffsetOnAxis(ap=x_idx[0:ROWS, :], axis=0),
                                        bounds_check=last_x, oob_is_err=False).then_inc(xg_in, 16)

            def scatter(col):
                steps(pool.tensor_copy(y_idx[0:ROWS, :], lists[0:ROWS, ds(col, 1)] if not isinstance(col, int) else lists[0:ROWS, col:col + 1]))
                steps.wait()
                pool.sem_inc(marks, 1)
                pool.indirect_dma_start(y_dram, bass.IndirectOffsetOnAxis(ap=y_idx[0:ROWS, :], axis=0), y_sb[0:ROWS, :], None,
                                        bounds_check=last_y, oob_is_err=False).then_inc(y_sent, 16)

            def send(s, col):
                pool.wait_ge(y_ok, s + 2)
                pool.sem_inc(marks, 1)
                scatter(col)

            def free_y(s):
                pool.wait_ge(y_sent, 16 * s + 16)
                pool.sem_inc(y_free, 1)

            pool.sem_inc(y_free, 1)
            pool.wait_ge(lists_x_ok, 1)
            pool.wait_ge(x2_stored, 16 * TT)
            gather(0)
            pool.wait_ge(xe_turned, 1)
            gather(1)
            pool.wait_ge(xe_turned, 2)
            gather(2)

            def rows_next(e, first_turn=None):
                pool.wait_ge(xe_turned, e + 3)
                pool.sem_inc(marks, 1)
                gather(e + 3)
                if first_turn is None:
                    free_y(e - 1)
                else:
                    with pool.If(first_turn > 0):
                        free_y(e - 1)
                send(e, e)

            with pool.Fori(0, PAIRS) as i:
                steps.enter(i, 4)
                for b in range(2):
                    rows_next(2 * i + b, None if b else i)
                steps.leave(PAIRS)
            rows_next(EXPERTS - 2)
            free_y(EXPERTS - 2)
            send(EXPERTS - 1, EXPERTS - 1)
            free_y(EXPERTS - 1)
            pool.wait_ge(ovf_ready, 1)
            n_over = pool.value_load(ovf_row[0:1, 32:33], min_val=0, max_val=MAX_OVERFLOW)
            with pool.If(n_over > 0):
                with pool.Fori(0, (MAX_OVERFLOW + 1) // 2) as i:
                    steps.enter(i, 4)
                    for b in range(2):
                        j = 2 * i + b
                        with pool.If(n_over > j):
                            col = pool.value_load(ovf_row[0:1, ds(j, 1)], min_val=0, max_val=LIST_COLS - 1)
                            pool.wait_ge(xe_turned, j + (EXPERTS + 1))
                            pool.wait_ge(xg_in, 16 * j + 16 * (EXPERTS + 2))
                            pool.sem_inc(marks, 1)
                            gather(col)
                            send(j + EXPERTS, col)
                            free_y(j + EXPERTS)
                    steps.leave((MAX_OVERFLOW + 1) // 2)
            pool.sem_inc(moe_done, 1)
            pool.wait_ge(x2a_ok, TT)
            for t in range(1, TT):
                pool.wait_ge(first_scaled, t)
                pool.tensor_tensor(x2[:, t, :], x2[:, t, :], y_rows[:, t, 0:D], ALU.add).then_inc(first_ok, 1)

        @block.scalar
        def _(act):
            def copy(dst, src):
                return act.activation(dst, src, ACT.Copy)

            def split_hi(u):
                act.wait_ge(loaded[u.slot], 16 * u.fill)
                act.wait_ge(units_done, u.n + 1)
                copy(w_hi[:, u.slot, :], raw[:, u.slot, :]).then_inc(hi_done, 1)

            def done(u):
                act.wait_ge(units_done, u.n + 1 + RING)

            act.sem_inc(tanh_ok, 3)
            act.sem_inc(sqrt_ok, 3)
            act.sem_inc(decay_ok, 3)
            for t in range(TT):
                act.dma_start(x_rows[:, t, :], x_view[t]).then_inc(x_in[t], 16)
            for k in range(KD):
                act.wait_ge(xt_turned, k + 1)
                copy(xt_hi[:, k, :], bank[:, k, :]).then_inc(xt_hi_ok, 1)
                if k == 3:
                    split_hi(Unit(U_LRU))
            for j in (1, 2):
                split_hi(Unit(U_LRU, j))
            act.wait_ge(lam_e, 1)
            act.activation(cur[:, 12:24], cur[:, 0:12], ACT.Exp, scale=-1.0).then_inc(lam_e, 1)

            def tail_gates(s, b):
                for j in range(3):
                    act.wait_ge(rg_done, 6 * s + 2 * j + 1 + 6)
                    act.activation(r_t[:, j, :], bank[:, j, :], ACT.Sigmoid, bias=cur_v[:, b, 5, j:j + 1]).then_inc(gates_ok, 1)
                    act.wait_ge(rg_done, 6 * s + 2 * j + 2 + 6)
                    act.activation(i_t[:, j, :], bank[:, (6, 7, 3)[j], :], ACT.Sigmoid, bias=cur_v[:, b, 6, j:j + 1]).then_inc(gates_ok, 1)

            def tail_decay(s, b):
                act.wait_ge(lru_split, 3 * s + 3)
                for j in range(3):
                    act.wait_ge(gates_ok, 6 * s + 2 * j + 1 + 6)
                    act.activation(s_t[:, j, :], r_t[:, j, :], ACT.Tanh, scale=cur_rate[:, 6 * b + j:6 * b + j + 1]).then_inc(tanh_ok, 1)
                for j in range(3):
                    act.wait_ge(tanh_ok, 3 * s + j + 1 + 3)
                    act.activation(r_t[:, j, :], r_t[:, j, :], ACT.Exp, scale=cur_rate[:, 6 * b + 3 + j:6 * b + 4 + j]).then_inc(decay_ok, 1)
                for j in range(3):
                    act.activation(s_t[:, j, :], s_t[:, j, :], ACT.Sqrt).then_inc(sqrt_ok, 1)

            def evict_u(s, b, j, u):
                done(u)
                act.wait_ge(tail_ok, 3 * s + j + 1)
                act.wait_ge(cur_ok, s + 1)
                copy(u_ext[:, j, 3:3 + TOKENS], bank[:, j, :])
                act.activation(conv[:, j, :], bank[:, j, :], ACT.Identity, bias=cur_v[:, b, 4, j:j + 1],
                               scale=cur_v[:, b, 3, j:j + 1]).then_inc(u_out, 1)

            with act.Fori(0, 2) as i:
                for half in range(2):
                    s = 2 * i + half
                    u = [Unit(U_LRU, 6 * half + j, i, 12) for j in range(6)]
                    split_hi(u[0].ahead(3))
                    if half:
                        tail_gates(s - 1, 0)
                        tail_decay(s - 1, 0)
                    else:
                        with act.If(i > 0):
                            tail_gates(s - 1, 1)
                            tail_decay(s - 1, 1)
                    split_hi(u[1].ahead(3))
                    split_hi(u[2].ahead(3))
                    evict_u(s, half, 0, u[0])
                    split_hi(u[3].ahead(3))
                    evict_u(s, half, 1, u[1])
                    evict_u(s, half, 2, u[2])
                    act.wait_ge(rg_in, 128 * s + 128)
                    act.wait_ge(rg_done, 6 * s + 6)
                    copy(rg_hi[:, :, :], rg_raw[:, :, :]).then_inc(rg_hi_ok, 1)
                    for j in range(3):
                        act.wait_ge(conv_ok, 3 * s + j + 1)
                        copy(conv_hi[:, j, :], conv[:, j, :]).then_inc(conv_hi_ok, 1)
                    split_hi(u[4].ahead(3))
                    for j in range(3):
                        if j == 2:
                            split_hi(u[5].ahead(3))
                        done(u[3 + j])
                        act.activation(gelu[:, j, :], bank[:, 3 + j, :], ACT.Gelu_apprx_tanh).then_inc(gelu_ok, 1)

            def grec(k):
                done(Unit(U_GREC, k))
                act.activation(merge[:, k, :], bank[:, 4 + k % 2, :], ACT.Sigmoid,
                               bias=vec[:, V_MERGE + KD + k:V_MERGE + KD + k + 1]).then_inc(grec_ok, 1)

            for k in range(KD):
                split_hi(Unit(U_GREC, k).ahead(3))
                if k == 0:
                    tail_gates(3, 1)
                    act.wait_ge(rg_split, 4 + 1)
                    act.wait_ge(rg_done, 24 + 6)
                if k == 1:
                    tail_decay(3, 1)
                grec(k)
            with act.Fori(0, 4) as i:
                for j in range(4):
                    split_hi(Unit(U_LO, j, i, 4).ahead(3))

            def hi_qk(h, a, b):
                for x in range(a, b):
                    act.wait_ge(roped, 4 * h + x + 1)
                    act.wait_ge(scored, 4 * h + 4)
                    copy(qk_hi[:, x, :], rope_o[:, x, :]).then_inc(qk_hi_ok, 1)

            def hi_ret(h):
                for j in range(4):
                    act.wait_ge(retf_ok, 4 * h + j + 1)
                    act.wait_ge(pv_ok, 4 * h + 8)
                    copy(ret_hi[:, j, :], gated[:, j, :]).then_inc(ret_hi_ok, 1)

            def act_qk(h, u, ret=None):
                for j in range(4):
                    split_hi(u.ahead(j + 3))
                    if j == 2:
                        hi_qk(h, 0, 2)
                        if ret is not None:
                            hi_ret(ret)
                hi_qk(h, 2, 4)

            def act_vg(h, u):
                for j in range(4):
                    split_hi(u.ahead(j + 3))
                done(u.ahead(3))
                act.wait_ge(pv_ok, 4 * h + 4)
                for t in range(TT):
                    copy(v_hi[:, t, :], bank[:, 4 + t, :]).then_inc(v_hi_ok, 1)
                at_p = 0
                for k in range(TT):
                    w = TOKENS - k * P
                    act.wait_ge(masked_ok, 4 * h + k + 1)
                    copy(p_hi[:, at_p:at_p + w], p_f[:, at_p:at_p + w]).then_inc(p_hi_ok, 1)
                    at_p += w
                act.wait_ge(ret_split, 4 * h + 4)
                for j in range(4):
                    split_hi(u.ahead(4 + j + 3))
                    done(u.ahead(4 + j))
                    act.activation(gated[:, j, :], bank[:, 4 + j, :], ACT.Silu).then_inc(silu_ok, 1)
                act.wait_ge(turned, 4 * h + 4)
                for t in range(TT):
                    act.wait_ge(var_ok, 4 * h + t + 1)
                    act.activation(scale_v[:, 0:1], mv[:, 1:2], ACT.Sqrt).then_inc(std_ok, 1)
                    act.wait_ge(rstd_ok, 4 * h + t + 1)
                    act.activation(normed[:, t, :], bank[:, t, :], ACT.Identity, bias=scale_v[:, 2:3], scale=scale_v[:, 1:2]).then_inc(normed_ok, 1)

            act_qk(0, Unit(U_QK0))
            with act.Fori(0, HEADS - 1) as h:
                act_vg(h, Unit(U_HEAD, 0, h, 16))
                act_qk(h + 1, Unit(U_HEAD, 8, h, 16), h)
                for j in range(4):
                    split_hi(Unit(U_HEAD, 12 + j, h, 16).ahead(3))
            act_vg(HEADS - 1, Unit(U_LAST))
            for k in range(KD):
                u = Unit(U_GRET, k)
                split_hi(u.ahead(3))
                done(u)
                act.wait_ge(p_split, 4 * HEADS)
                act.activation(g_ret[:, k, :], bank[:, k % 4, :], ACT.Sigmoid, bias=vec[:, V_MERGE + k:V_MERGE + k + 1]).then_inc(gret_ok, 1)
                if k == 3:
                    hi_ret(HEADS - 1)

            def split_out_hi(n):
                if n < U_OUT:
                    return split_hi(Unit(n))
                u = Unit(n)
                act.wait_ge(loaded[u.slot], 16 * u.fill)
                act.wait_ge(units_done, U_RET3 + RING)
                copy(wo_hi[:, n - U_OUT, :], raw[:, u.slot, :]).then_inc(hi_done, 1)

            nxt = U_RET3 + 3
            for j in range(4):
                for _ in range(3 if j == 0 else 2):
                    split_out_hi(nxt)
                    nxt += 1
                for k in (2 * j, 2 * j + 1):
                    act.wait_ge(merged, k + 1)
                    act.wait_ge(ret_split, 4 * HEADS + 4)
                    act.wait_ge(turned, 4 * HEADS + 4)
                    copy(mrg_hi[:, k, :], acc[:, k, :]).then_inc(mrg_hi_ok, 1)
            assert nxt == U_END

            def x2t_out(t):
                act.wait_ge(x2_turned, t + 1)
                if t >= 2:
                    act.wait_ge(routed, t - 1)
                if t == 0:
                    act.wait_ge(qk_split, 4 * HEADS)
                copy(x2_t[:, t % 2, :].rearrange("p (b n) -> p b n", b=2), bank[:, 4:6, :]).then_inc(x2t_ok, 1)

            for t in range(TT):
                if t:
                    x2t_out(t - 1)
                act.wait_ge(x2_var, t + 1)
                act.activation(scale_v[:, 0:1], mv[:, 1:2], ACT.Sqrt).then_inc(x2_std, 1)
            x2t_out(TT - 1)
            act.wait_ge(exp_ok, 1)
            act.activation(res[:, 8:28], res[:, 8:28], ACT.Exp).then_inc(exp_ok, 1)
            act.wait_ge(x2_stored, 16 * TT)
            for t in range(TT):
                act.activation(x2[:, t, :], x2[:, t, :], ACT.Copy, scale=ALPHA).then_inc(x2a_ok, 1)

            def m_hi_part(u):
                act.wait_ge(m_loaded[u.slot], 16 * u.fill)
                act.wait_ge(m_done, u.n + 1)
                copy(m_hi[:, u.slot % MSPLIT, :], m_raw[u.slot][:, :]).then_inc(m_hi_ok, 1)

            def m_finished(u):
                act.wait_ge(m_done, u.n + 1 + MSPLIT)

            def xe_hi_part(s):
                act.wait_ge(xe_turned, s + 1)
                copy(xe_hi[:, :, 0:ROWS], bank_x[:, :, 0:ROWS]).then_inc(xe_hi_ok, 1)

            def ht_hi_part(s):
                act.wait_ge(h_turned, s + 1)
                copy(ht_hi[:, :, 0:ROWS], bank_h[:, :, 0:ROWS]).then_inc(ht_hi_ok, 1)

            def silu_part(s, u):
                m_finished(u)
                act.activation(silu[:, :], bank[:, 0, :], ACT.Silu).then_inc(m_silu, 1)

            def y_out(s, u):
                m_finished(u)
                act.wait_ge(y_free, s + 1)
                copy(y_sb[:, :].rearrange("p (b n) -> p b n", b=2), bank[:, 2:4, :]).then_inc(y_ok, 1)

            u = Unit(0, ring=MRING)
            act.wait_ge(proj_ok, TT)
            act.wait_ge(consts_ok, 1)
            for tile in (xe_hi, xe_lo, ht_hi, ht_lo):
                n = tile.shape[1]
                act.activation(tile[:, :, ROWS:P], ident[:, 0:P - ROWS].unsqueeze(1).to_broadcast([P, n, P - ROWS]), ACT.Copy, scale=0.0)
            m_hi_part(u)
            m_hi_part(u.ahead(1))
            xe_hi_part(0)
            for j in range(4):
                if j == 2:
                    silu_part(0, u.ahead(1))
                m_hi_part(u.ahead(j + 2))
            xe_hi_part(1)

            def act_next(e, u):
                m_hi_part(u.ahead(2))
                ht_hi_part(e)
                m_hi_part(u.ahead(3))
                m_hi_part(u.ahead(4))
                silu_part(e + 1, u.ahead(1))
                m_hi_part(u.ahead(5))
                m_hi_part(u.ahead(6))
                xe_hi_part(e + 2)
                m_hi_part(u.ahead(7))
                y_out(e, u.ahead(5))

            with act.Fori(0, PAIRS) as i:
                for b in range(2):
                    act_next(2 * i + b, Unit(4 + 6 * b, 0, i, 12, MRING))
            act_next(EXPERTS - 2, Unit(4 + 12 * PAIRS, ring=MRING))
            ht_hi_part(EXPERTS - 1)
            y_out(EXPERTS - 1, Unit(M_LAST, 1, ring=MRING))
            act.wait_ge(ovf_ready, 1)
            n_over = act.value_load(ovf_row[0:1, 32:33], min_val=0, max_val=MAX_OVERFLOW)
            with act.If(n_over > 0):
                with act.Fori(0, (MAX_OVERFLOW + 1) // 2) as i:
                    for b in range(2):
                        j = 2 * i + b
                        with act.If(n_over > j):
                            u = Unit(M_END + 6 * b, 0, i, 12, MRING)
                            xe_hi_part(j + (EXPERTS + 1))
                            for k in range(4):
                                m_hi_part(u.ahead(k))
                            silu_part(j + EXPERTS, u.ahead(1))
                            ht_hi_part(j + EXPERTS)
                            m_hi_part(u.ahead(4))
                            m_hi_part(u.ahead(5))
                            y_out(j + EXPERTS, u.ahead(5))
            def scale_first(t):
                act.wait_ge(rows_in[t], 16)
                act.activation(y_rows[:, t, 0:D], y_rows[:, t, 0:D], ACT.Identity, scale=wts[:, 2 * t:2 * t + 1]).then_inc(first_scaled, 1)

            scale_first(1)
            for t in range(TT):
                if 1 <= t < TT - 1:
                    scale_first(t + 1)
                act.wait_ge(f_var, t + 1)
                act.activation(scale_v[:, 0:1], mv[:, 1:2], ACT.Sqrt).then_inc(f_std, 1)

        @block.vector
        def _(dve):
            step = Steps(dve, dve_steps)

            def tt(dst, a, b, op):
                return dve.tensor_tensor(dst, a, b, op)

            def sub(dst, a, b_r):
                return dve.tensor_tensor(dst, a, b_r.bitcast(F32), ALU.subtract)

            def split_lo(u):
                dve.wait_ge(hi_done, u.n + 1)
                sub(w_lo[:, u.slot, :], raw[:, u.slot, :], w_hi[:, u.slot, :]).then_inc(split_done, 1)

            def done(u):
                dve.wait_ge(units_done, u.n + 1 + RING)

            dve.sem_inc(split_done, RING)
            dve.sem_inc(rg_split, 1)
            dve.sem_inc(tail_ok, 3)
            dve.sem_inc(lru_split, 3)
            dve.sem_inc(lo_ok, 2)
            dve.sem_inc(ret_split, 4)
            dve.sem_inc(ret_out, 8)
            dve.sem_inc(m_split_ok, MRING)
            dve.wait_ge(vec_turned, 1)
            dve.tensor_copy(vec[:, :], bank[:, 7, 0:V_ROWS]).then_inc(vec_ready, 1)
            for k in range(KD):
                dve.wait_ge(xt_hi_ok, k + 1)
                sub(xt_lo[:, k, :], bank[:, k, :], xt_hi[:, k, :]).then_inc(xt_split, 1)
                if k == 3:
                    split_lo(Unit(U_LRU))
            step(dve.memset(u_ext[:, :, 0:3], 0.0))
            step.wait()
            for j in (1, 2):
                split_lo(Unit(U_LRU, j))

            dve.wait_ge(vec_ready, 1)
            lam, mag, e, s, s2, q = vec[:, V_LAM:V_LAM + 12], cur[:, 0:12], cur[:, 12:24], cur[:, 24:36], inv[:, 0:12], inv[:, 12:24]
            neg = inv[:, 24:36]
            step(dve.tensor_scalar(neg, lam, -1.0, None, ALU.mult))
            step.wait()
            tt(mag, lam, neg, ALU.max).then_inc(lam_e, 1)
            dve.wait_ge(lam_e, 2)
            step(dve.tensor_scalar(q, e, 2.0, None, ALU.add))
            step.wait()
            step(dve.reciprocal(s, q))
            step.wait()
            step(tt(s, s, e, ALU.mult))
            step.wait()
            step(tt(s2, s, s, ALU.mult))
            step.wait()
            step(dve.tensor_scalar(q, s2, 1.0 / 19, None, ALU.mult))
            for k in range(8, 0, -1):
                step.wait()
                step(dve.scalar_tensor_tensor(q, q, 1.0 / (2 * k + 1), s2, ALU.add, ALU.mult))
            step.wait()
            step(dve.scalar_tensor_tensor(q, q, 1.0, s, ALU.add, ALU.mult))
            step(dve.tensor_scalar(neg, neg, 0.0, 4.0, ALU.max, ALU.mult))
            step.wait()
            dve.scalar_tensor_tensor(rate[:, :], q, 8.0, neg, ALU.mult, ALU.add).then_inc(rate_ok, 1)
            dve.wait_ge(rate_ok, 1)

            def tail(s, j):
                r, iv, sq = r_t[:, j, :], i_t[:, j, :], s_t[:, j, :]
                dve.wait_ge(gates_ok, 6 * s + 2 * j + 2 + 6)
                step(tt(iv, iv, conv[:, j, :], ALU.mult))
                dve.wait_ge(sqrt_ok, 3 * s + j + 1 + 3)
                dve.wait_ge(decay_ok, 3 * s + j + 1 + 3)
                step(dve.scalar_tensor_tensor(sq, r, 1.0, sq, ALU.add, ALU.mult))
                step.wait()
                step(tt(iv, iv, sq, ALU.mult))
                step.wait()
                step(dve.tensor_tensor_scan(sq, r, iv, 0.0, ALU.mult, ALU.add))
                step.wait()
                dve.wait_ge(gelu_ok, 3 * s + j + 1 + 3)
                tt(sq, sq, gelu[:, j, :], ALU.mult).then_inc(tail_ok, 1)

            def lru_parts(s):
                dve.wait_ge(tail_ok, 3 * s + 6)
                if not isinstance(s, int):
                    s = nc.s_assert_within(s, 0, 3, skip_runtime_bounds_check_because="runs for blocks 0 to 3 only")
                for j in range(3):
                    k = 3 * s + j
                    at_k = slice(k, k + 1) if isinstance(k, int) else ds(k, 1)
                    h, lo = lru_hi[:, at_k, :].rearrange("p a n -> p (a n)"), lru_lo[:, at_k, :].rearrange("p a n -> p (a n)")
                    step(dve.tensor_scalar(h, s_t[:, j, :], 1.0, None, ALU.mult))
                    step.wait()
                    sub(lo, s_t[:, j, :], h).then_inc(lru_split, 1)

            def conv_tile(s, b, j):
                dve.wait_ge(u_out, 3 * s + j + 1)
                for tap in (2, 1):
                    step(dve.scalar_tensor_tensor(conv[:, j, :], u_ext[:, j, tap:tap + TOKENS], cur_v[:, b, tap, j:j + 1],
                                                  conv[:, j, :], ALU.mult, ALU.add))
                    step.wait()
                dve.scalar_tensor_tensor(conv[:, j, :], u_ext[:, j, 0:TOKENS], cur_v[:, b, 0, j:j + 1],
                                         conv[:, j, :], ALU.mult, ALU.add).then_inc(conv_ok, 1)

            vec_k = vec[:, 0:84].rearrange("p (k t) -> p k t", t=WT)

            def block_vectors(s, b):
                step(dve.tensor_scalar(cur_rate[:, 6 * b:6 * b + 3], rate[:, ds(3 * s, 3)], 1.0, None, ALU.mult))
                step(dve.tensor_scalar(cur_rate[:, 6 * b + 3:6 * b + 6], rate[:, ds(3 * s, 3)], -2.0, None, ALU.mult))
                step.wait()
                dve.tensor_scalar(cur_v[:, b, :, :], vec_k[:, :, ds(3 * s, 3)], 1.0, None, ALU.mult).then_inc(cur_ok, 1)

            def lru_slots(i, half):
                s = 2 * i + half
                u = [Unit(U_LRU, 6 * half + j, i, 12) for j in range(6)]
                split_lo(u[0].ahead(3))
                block_vectors(s, half)
                for j in range(3):
                    if half:
                        tail(s - 1, j)
                    else:
                        with dve.If(i > 0):
                            before = step.done
                            tail(s - 1, j)
                        with dve.Else():
                            dve.sem_inc(dve_steps, step.done - before)
                    split_lo(u[1 + j].ahead(3))
                    if j == 1:
                        dve.wait_ge(cur_ok, s + 1)
                        conv_tile(s, half, 0)
                conv_tile(s, half, 1)
                conv_tile(s, half, 2)
                dve.wait_ge(rg_hi_ok, s + 1)
                sub(rg_lo[:, :, :], rg_raw[:, :, :], rg_hi[:, :, :]).then_inc(rg_split, 1)
                for j in range(3):
                    dve.wait_ge(conv_hi_ok, 3 * s + j + 1)
                    sub(conv_lo[:, j, :], conv[:, j, :], conv_hi[:, j, :]).then_inc(conv_split, 1)
                split_lo(u[4].ahead(3))
                split_lo(u[5].ahead(3))
                if half:
                    lru_parts(s - 1)
                else:
                    with dve.If(i > 0):
                        before = step.done
                        lru_parts(s - 1)
                    with dve.Else():
                        dve.sem_inc(dve_steps, step.done - before)

            per = 2 * (2 + 3 * 4 + 3 * 2 + 3)
            with dve.Fori(0, 2) as i:
                step.enter(i, per)
                lru_slots(i, 0)
                lru_slots(i, 1)
                step.leave(2)
            for k in range(KD):
                split_lo(Unit(U_GREC, k).ahead(3))
                if 1 <= k <= 3:
                    tail(3, k - 1)
                if k == 4:
                    lru_parts(3)
            dve.wait_ge(grec_ok, KD)
            with dve.Fori(0, 4) as i:
                for cc in range(2):
                    for j in range(2):
                        split_lo(Unit(U_LO, 2 * cc + j, i, 4).ahead(3))
                    done(Unit(U_LO, 2 * cc + 1, i, 4))
                    m = merge[:, ds(2 * i + cc, 1), :].rearrange("p a n -> p (a n)")
                    tt(m, m, bank[:, cc, :], ALU.mult).then_inc(lo_ok, 1)

            def rotate(h, a):
                cos, sin = rope[:, 0, :], rope[:, 1, :]
                for x, (f, g, op) in enumerate(((cos, sin, ALU.subtract), (sin, cos, ALU.add))):
                    if not (isinstance(h, int) and h == 0 and a + x == 0):
                        dve.wait_ge(roped, 4 * h + a + x)
                    step(tt(rope_a[:, :], bank[:, a, :], f, ALU.mult))
                    step(tt(rope_b[:, :], bank[:, a + 1, :], g, ALU.mult))
                    step.wait()
                    tt(rope_o[:, a + x, :], rope_a[:, :], rope_b[:, :], op).then_inc(roped, 1)

            def lo_qk(h, a):
                for x in (a, a + 1):
                    dve.wait_ge(qk_hi_ok, 4 * h + x + 1)
                    sub(qk_lo[:, x, :], rope_o[:, x, :], qk_hi[:, x, :]).then_inc(qk_split, 1)

            def ret_turned(h):
                for j in range(4):
                    dve.wait_ge(turned, 4 * h + j + 1 + 4)
                    tt(gated[:, j, :], bank[:, 4 + j, :], gated[:, j, :], ALU.mult).then_inc(retf_ok, 1)

            def lo_ret(h):
                for j in range(4):
                    dve.wait_ge(ret_hi_ok, 4 * h + j + 1)
                    sub(ret_lo[:, j, :], gated[:, j, :], ret_hi[:, j, :]).then_inc(ret_split, 1)

            def dve_qk(h, u, ret=None):
                split_lo(u.ahead(3))
                split_lo(u.ahead(4))
                done(u.ahead(1))
                if ret is None:
                    step(dve.memset(acc[:, :, :], 0.0))
                    step.wait()
                rotate(h, 0)
                split_lo(u.ahead(5))
                lo_qk(h, 0)
                if ret is not None:
                    ret_turned(ret)
                    lo_ret(ret)
                split_lo(u.ahead(6))
                done(u.ahead(3))
                rotate(h, 2)
                lo_qk(h, 2)

            def dve_vg(h, u):
                for j in range(4):
                    split_lo(u.ahead(j + 3))
                for t in range(TT):
                    dve.wait_ge(v_hi_ok, 4 * h + t + 1)
                    sub(v_lo[:, t, :], bank[:, 4 + t, :], v_hi[:, t, :]).then_inc(v_split, 1)
                d = decay[:, h, :] if isinstance(h, int) else decay[:, ds(h, 1), :].rearrange("p a n -> p (a n)")
                spans, at_p = [], 0
                for k in range(TT):
                    spans.append((at_p, at_p + TOKENS - k * P))
                    at_p = spans[-1][1]
                for k, (a, b) in enumerate(spans):
                    dve.wait_ge(scored, 4 * h + k + 1 + 4)
                    tt(p_f[:, a:b], bank[:, k, 0:b - a], d[:, 0:b - a], ALU.mult).then_inc(masked_ok, 1)
                for k, (a, b) in enumerate(spans):
                    dve.wait_ge(p_hi_ok, 4 * h + k + 1)
                    sub(p_lo[:, a:b], p_f[:, a:b], p_hi[:, a:b]).then_inc(p_split, 1)
                for j in range(4):
                    split_lo(u.ahead(4 + j + 3))
                for t in range(TT):
                    dve.wait_ge(pv_ok, 4 * h + t + 1 + 4)
                    moments([bank[:, t, :]], var_ok, std_ok, rstd_ok, 4 * h + t + 1)

            def moments(parts, var, std, rstd, n):
                for x, part_ap in enumerate(parts):
                    step(dve.bn_stats(stats[:, 6 * x:6 * x + 6], part_ap))
                step.wait()
                dve.sem_inc(marks, 1)
                step(dve.bn_aggr(mv[:, :], stats[:, 0:6 * len(parts)]))
                step.wait()
                dve.tensor_scalar(mv[:, 1:2], mv[:, 1:2], EPS, None, ALU.add).then_inc(var, 1)
                dve.wait_ge(std, n)
                step(dve.reciprocal(scale_v[:, 1:2], scale_v[:, 0:1]))
                step.wait()
                dve.scalar_tensor_tensor(scale_v[:, 2:3], mv[:, 0:1], -1.0, scale_v[:, 1:2], ALU.mult, ALU.mult).then_inc(rstd, 1)
                dve.wait_ge(rstd, n)

            dve.wait_ge(tables_in, 32)
            dve_qk(0, Unit(U_QK0))
            per = 4 * 3 + 8
            with dve.Fori(0, HEADS - 1) as h:
                step.enter(h, per)
                dve_vg(h, Unit(U_HEAD, 0, h, 16))
                dve_qk(h + 1, Unit(U_HEAD, 8, h, 16), h)
                for j in range(4):
                    u = Unit(U_HEAD, 12 + j, h, 16)
                    split_lo(u.ahead(3))
                    done(u)
                    for k in (2 * j, 2 * j + 1):
                        dve.wait_ge(ret_out, 8 * h + k + 1)
                        tt(acc[:, k, :], acc[:, k, :], bank[:, 4 + k % 4, :], ALU.add).then_inc(ret_out, 1)
                step.leave(HEADS - 1)
            dve_vg(HEADS - 1, Unit(U_LAST))
            for k in range(KD):
                split_lo(Unit(U_GRET, k).ahead(3))
                if k == 3:
                    ret_turned(HEADS - 1)
                if k == 4:
                    lo_ret(HEADS - 1)

            def split_out_lo(n):
                u = Unit(n)
                dve.wait_ge(hi_done, n + 1)
                if n < U_OUT:
                    sub(w_lo[:, u.slot, :], raw[:, u.slot, :], w_hi[:, u.slot, :]).then_inc(split_done, 1)
                else:
                    sub(wo_lo[:, n - U_OUT, :], raw[:, u.slot, :], wo_hi[:, n - U_OUT, :]).then_inc(split_done, 1)

            nxt = U_RET3 + 3
            dve.wait_ge(gret_ok, KD)
            for j in range(4):
                for _ in range(3 if j == 0 else 2):
                    split_out_lo(nxt)
                    nxt += 1
                done(Unit(U_RET3 + j))
                pair = (2 * j, 2 * j + 1)
                for k in pair:
                    dve.wait_ge(acc_ok, k + 1)
                    tt(g_ret[:, k, :], g_ret[:, k, :], bank[:, 4 + k % 4, :], ALU.mult).then_inc(ret_out, 1)
                for k in pair:
                    dve.wait_ge(ret_out, 8 * HEADS + k + 1)
                    tt(acc[:, k, :], acc[:, k, :], g_ret[:, k, :], ALU.add).then_inc(merged, 1)
                for k in pair:
                    dve.wait_ge(mrg_hi_ok, k + 1)
                    sub(mrg_lo[:, k, :], acc[:, k, :], mrg_hi[:, k, :]).then_inc(mrg_split, 1)

            dve.wait_ge(res_in, 16)
            dve.wait_ge(ln1_in, 32)

            def layer_norm(t, ln, var, std, ok):
                xt = x2[:, t, :]
                for half in range(2):
                    step(dve.bn_stats(stats[:, 6 * half:6 * half + 6], x2[:, t, 512 * half:512 * half + 512]))
                step.wait()
                step(dve.bn_aggr(mv[:, :], stats[:, :]))
                step.wait()
                dve.tensor_scalar(mv[:, 1:2], mv[:, 1:2], EPS, None, ALU.add).then_inc(var, 1)
                step(dve.scalar_tensor_tensor(xt, xt, mv[:, 0:1], ln[:, 0, :], ALU.subtract, ALU.mult))
                dve.wait_ge(std, t + 1)
                step(dve.reciprocal(scale_v[:, 1:2], scale_v[:, 0:1]))
                step.wait()
                dve.scalar_tensor_tensor(xt, xt, scale_v[:, 1:2], ln[:, 1, :], ALU.mult, ALU.add).then_inc(ok, 1)

            for t in range(TT):
                dve.wait_ge(proj_ok, t + 1)
                for half in range(2):
                    c0, c1 = 512 * half, 512 * half + 512
                    dve.scalar_tensor_tensor(x2[:, t, c0:c1], x_res[:, t, c0:c1], ALPHA, bank[:, 2 * (t % 2) + half, :],
                                             ALU.mult, ALU.add).then_inc(z_ok, 1)
                dve.wait_ge(z_ok, 2 * t + 2)
                layer_norm(t, ln1, x2_var, x2_std, x2_ok)

            dve.wait_ge(router_in, 64)
            dve.wait_ge(consts_ok, 1)
            dve.wait_ge(routed, TT)
            lg = logit[:, :].rearrange("p (t n) -> p t n", t=TT)
            step(tt(lg, bank[:, 6, 0:TT * 36].rearrange("p (t n) -> p t n", t=TT),
                    b_rt[:, :].unsqueeze(1).to_broadcast([P, TT, 36]), ALU.add))
            step.wait()

            def wide(ap, n):
                return ap.unsqueeze(2).to_broadcast([P, TT, n])

            def first_max(vals, n, iota, best, hot):
                v3 = vals
                h3 = hot.rearrange("p (t n) -> p t n", t=TT)
                step(dve.tensor_reduce(best, v3, AX, ALU.max))
                step.wait()
                step(tt(h3, v3, wide(best, n), ALU.is_ge))
                step.wait()
                it = iota[:, :].unsqueeze(1).to_broadcast([P, TT, n])
                step(tt(h3, h3, it, ALU.mult))
                step.wait()
                step(dve.tensor_reduce(red[:, :], h3, AX, ALU.min))
                step.wait()
                step(tt(h3, it, wide(red[:, :], n), ALU.is_equal))
                step.wait()

            best_g, best_1, best_2 = res[:, 0:4], res[:, 4:8], res[:, 28:32]
            diff, exps = res[:, 8:12], res[:, 12:28]
            first_max(lg[:, :, 0:4], 4, iota_g, best_g, hot_g[:, :])
            step(tt(exps.rearrange("p (t n) -> p t n", t=TT), lg[:, :, 0:4], wide(best_g, 4), ALU.subtract))
            m4 = masked[:, :].rearrange("p (t g e) -> p t g e", t=TT, g=GROUPS)
            hg = hot_g[:, :].rearrange("p (t g) -> p t g", t=TT)
            for t in range(TT):
                step(tt(m4[:, t], lg[:, t, 4:36].rearrange("p (g e) -> p g e", g=GROUPS),
                        hg[:, t, :].unsqueeze(2).to_broadcast([P, GROUPS, PER_GROUP]), ALU.mult))
            step.wait()
            e3 = e8[:, :].rearrange("p (t e) -> p t e", t=TT)
            for t in range(TT):
                step(dve.tensor_reduce(e3[:, t, :], m4[:, t].rearrange("p g e -> p e g"), AX, ALU.add))
            step.wait()
            first_max(e3, PER_GROUP, iota_e, best_1, hot_1[:, :])
            step(dve.scalar_tensor_tensor(e8[:, :], hot_1[:, :], -3.0e38, e8[:, :], ALU.mult, ALU.add))
            step.wait()
            first_max(e3, PER_GROUP, iota_e, best_2, hot_2[:, :])
            tt(diff, best_2, best_1, ALU.subtract).then_inc(exp_ok, 1)
            for t in range(TT):
                for mem, hot in ((mem0, hot_1), (mem1, hot_2)):
                    step(tt(mem[:, 32 * t:32 * t + 32].rearrange("p (g e) -> p g e", g=GROUPS),
                            hg[:, t, :].unsqueeze(2).to_broadcast([P, GROUPS, PER_GROUP]),
                            hot[:, 8 * t:8 * t + 8].unsqueeze(1).to_broadcast([P, GROUPS, PER_GROUP]), ALU.mult))
            step.wait()
            tt(mem_bf[:, :], mem0[:, :], mem1[:, :], ALU.add).then_inc(members_ok, 1)
            dve.wait_ge(exp_ok, 2)
            step(dve.tensor_reduce(red[:, :], exps.rearrange("p (t n) -> p t n", t=TT), AX, ALU.add))
            step.wait()
            step(dve.scalar_tensor_tensor(red[:, :], diff, 1.0, red[:, :], ALU.add, ALU.mult))
            step.wait()
            wt = wts[:, :].rearrange("p (t k) -> p t k", k=2)
            step(dve.reciprocal(wt[:, :, 0], red[:, :]))
            step.wait()
            step(tt(wt[:, :, 1], wt[:, :, 0], diff, ALU.mult))
            dve.wait_ge(ranked, 1)
            rank = bank[:, 7, 0:TT * 32]
            af = addr_f[:, :]
            m3 = masked[:, :].rearrange("p (t e) -> p t e", t=TT)
            me3 = masked_e[:, :].rearrange("p (t e) -> p t e", t=TT)
            exp_row = over_c[:, 0:32]
            slot = af[:, 0:8].rearrange("p (t k) -> p t k", k=2)
            eidx = af[:, 8:16].rearrange("p (t k) -> p t k", k=2)
            for k, mem in enumerate((mem0, mem1)):
                mm = mem[:, :].rearrange("p (t e) -> p t e", t=TT)
                step(tt(masked[:, :], mem[:, :], rank, ALU.mult))
                step(tt(me3, mm, exp_row.unsqueeze(1).to_broadcast([P, TT, 32]), ALU.mult))
                step.wait()
                step(dve.tensor_reduce(slot[:, :, k], m3, AX, ALU.add))
                step(dve.tensor_reduce(eidx[:, :, k], me3, AX, ALU.add))
                step.wait()
            rows_log, cols_log, exp_log = (n.bit_length() - 1 for n in (ROWS, LIST_COLS, EXPERTS))
            si, in_blk, blk = slot_i[:, 0:8], slot_i[:, 8:16], slot_i[:, 16:24]
            step(dve.tensor_copy(si, af[:, 0:8]))
            step.wait()
            step(dve.tensor_scalar(in_blk, si, ROWS - 1, cols_log, ALU.bitwise_and, ALU.logical_shift_left))
            step(dve.tensor_scalar(blk, si, rows_log, exp_log, ALU.logical_shift_right, ALU.logical_shift_left))
            step.wait()
            step(tt(si, in_blk, blk, ALU.add))
            step.wait()
            dve.scalar_tensor_tensor(addr[:, :], af[:, 8:16], -float(EXPERTS), si, ALU.add, ALU.add).then_inc(addr_ok, 1)
            total = bank[:, 7, 128:160]
            for b in range(BLOCKS - 1):
                step(dve.tensor_scalar(over[:, 32 * b:32 * b + 32], total, float(ROWS * (b + 1)), None, ALU.is_gt))
            step.wait()
            step(dve.memset(over_s[:, :], 0.0))
            step.wait()
            step(dve.tensor_tensor_scan(over_r[:, :], over[:, :], over_s[:, :], 0.0, ALU.add, ALU.add))
            step.wait()
            step(dve.tensor_copy(ovf_row[:, 32:33], over_r[:, OVER - 1:OVER]))
            step(tt(over_s[:, :], over_r[:, :], over[:, :], ALU.subtract))
            step.wait()
            step(dve.scalar_tensor_tensor(over_s[:, :], over_s[:, :], part[:, :], over[:, :], ALU.is_equal, ALU.mult))
            step.wait()
            step(tt(over_s[:, :], over_s[:, :], over_c[:, :], ALU.mult))
            step.wait()
            dve.tensor_reduce(ovf_col[:, :], over_s[:, :], AX, ALU.add).then_inc(ovf_ok, 1)
            dve.wait_ge(ovf_turned, 1)
            step(dve.tensor_copy(ovf_row[0:1, 0:16], bank[0:1, 7, 256:272]))
            step.wait()
            dve.tensor_scalar(ovf_row[0:1, 16:32], ovf_row[0:1, 0:16], EXPERTS - 1, None, ALU.bitwise_and).then_inc(ovf_ready, 1)

            dve.wait_ge(lists_in, 16)
            dve.tensor_scalar(lists_x[0:ROWS, :], lists[0:ROWS, :], 1, None, ALU.logical_shift_right).then_inc(lists_x_ok, 1)

            def m_lo_part(u):
                dve.wait_ge(m_hi_ok, u.n + 1)
                sub(m_lo[:, u.slot % MSPLIT, :], m_raw[u.slot][:, :], m_hi[:, u.slot % MSPLIT, :]).then_inc(m_split_ok, 1)

            def xe_lo_part(s):
                dve.wait_ge(xe_hi_ok, s + 1)
                sub(xe_lo[:, :, 0:ROWS], bank_x[:, :, 0:ROWS], xe_hi[:, :, 0:ROWS]).then_inc(xe_split, 1)

            def ht_lo_part(s):
                dve.wait_ge(ht_hi_ok, s + 1)
                sub(ht_lo[:, :, 0:ROWS], bank_h[:, :, 0:ROWS], ht_hi[:, :, 0:ROWS]).then_inc(ht_split, 1)

            def h_part(s, u):
                dve.wait_ge(m_done, u.n + 1 + MSPLIT)
                dve.wait_ge(m_silu, s + 1)
                tt(h_sb[:, :], bank[:, 1, :], silu[:, :], ALU.mult).then_inc(h_ok, 1)

            u = Unit(0, ring=MRING)
            m_lo_part(u)
            m_lo_part(u.ahead(1))
            xe_lo_part(0)
            for j in range(4):
                m_lo_part(u.ahead(j + 2))
            h_part(0, u.ahead(3))
            xe_lo_part(1)

            def dve_next(e, u):
                m_lo_part(u.ahead(2))
                ht_lo_part(e)
                for j in range(3, 6):
                    m_lo_part(u.ahead(j))
                h_part(e + 1, u.ahead(3))
                m_lo_part(u.ahead(6))
                xe_lo_part(e + 2)
                m_lo_part(u.ahead(7))

            with dve.Fori(0, PAIRS) as i:
                for b in range(2):
                    dve_next(2 * i + b, Unit(4 + 6 * b, 0, i, 12, MRING))
            dve_next(EXPERTS - 2, Unit(4 + 12 * PAIRS, ring=MRING))
            ht_lo_part(EXPERTS - 1)
            n_over = dve.value_load(ovf_row[0:1, 32:33], min_val=0, max_val=MAX_OVERFLOW)
            with dve.If(n_over > 0):
                with dve.Fori(0, (MAX_OVERFLOW + 1) // 2) as i:
                    for b in range(2):
                        j = 2 * i + b
                        with dve.If(n_over > j):
                            u = Unit(M_END + 6 * b, 0, i, 12, MRING)
                            xe_lo_part(j + (EXPERTS + 1))
                            for k in range(4):
                                m_lo_part(u.ahead(k))
                            h_part(j + EXPERTS, u.ahead(3))
                            ht_lo_part(j + EXPERTS)
                            m_lo_part(u.ahead(4))
                            m_lo_part(u.ahead(5))

            dve.wait_ge(x2a_ok, TT)
            dve.wait_ge(ln2_in, 32)
            for t in range(TT):
                dve.wait_ge(rows_in[t], 16)
                if t:
                    dve.wait_ge(first_ok, t)
                for k in ((0, 1) if t == 0 else (1,)):
                    step(dve.scalar_tensor_tensor(x2[:, t, :], y_rows[:, t, D * k:D * k + D], wts[:, 2 * t + k:2 * t + k + 1],
                                                  x2[:, t, :], ALU.mult, ALU.add))
                    step.wait()
                layer_norm(t, ln2, f_var, f_std, f_ok)

        @block.tensor
        def _(pe):
            def products(dst, pairs, first=True, last=True):
                n = len(pairs)
                for x, (sh, sl, mh, ml) in enumerate(pairs):
                    pe.matmul(dst, sh, mh, start=first and x == 0, stop=False)
                    pe.matmul(dst, sh, ml, start=False, stop=False)
                    ins = pe.matmul(dst, sl, mh, start=False, stop=last and x == n - 1)
                return ins

            def ready(u):
                pe.wait_ge(split_done, u.n + 1 + RING)

            def cols_unit(u, b, splitting=False):
                ready(u)
                for k in range(KD):
                    if splitting:
                        pe.wait_ge(xt_split, k + 1)
                    last = products(bank[:, b, :], [(w_hi[:, u.slot, P * k:P * k + P], w_lo[:, u.slot, P * k:P * k + P],
                                                     xt_hi[:, k, :], xt_lo[:, k, :])], k == 0, k == KD - 1)
                last.then_inc(units_done, 1)

            pe.sem_inc(units_done, RING)
            pe.sem_inc(rg_done, 6)
            pe.sem_inc(scored, 4)
            pe.sem_inc(pv_ok, 4)
            pe.sem_inc(turned, 4)
            pe.sem_inc(m_done, MSPLIT)
            pe.sem_inc(gates_ok, 6)
            pe.sem_inc(gelu_ok, 3)
            pe.sem_inc(normed_ok, 4)
            pe.sem_inc(y_ok, 1)
            pe.wait_ge(ident_ok, 2)
            pe.wait_ge(vec_in, 96)
            pe.transpose(bank[:, 7, 0:V_ROWS], vec_rows[0:V_ROWS, :], ident[0:V_ROWS, 0:V_ROWS]).then_inc(vec_turned, 1)
            for k in range(KD):
                for t in range(TT):
                    if k == 0:
                        pe.wait_ge(x_in[t], 16)
                    if k == 7 and t == 0:
                        pe.wait_ge(vec_ready, 1)
                    last = pe.transpose(bank[:, k, P * t:P * t + P], x_rows[:, t, P * k:P * k + P], ident[:, :])
                last.then_inc(xt_turned, 1)
            pe.wait_ge(xt_split, 3)

            def rg_tiles(s):
                pe.wait_ge(rg_split, s + 2)
                pe.wait_ge(conv_split, 3 * s + 3)
                where = {(0, 0): 0, (1, 0): 128, (0, 1): 256, (1, 1): 384, (2, 1): 512, (1, 2): 640, (2, 2): 768}
                for o, ins_t in enumerate(((0, 1), (0, 1, 2), (1, 2))):
                    for g, b in ((0, o), (1, (6, 7, 3)[o])):
                        if g == 0:
                            pe.wait_ge(u_out, 3 * s + o + 1)
                        elif o == 2:
                            pe.wait_ge(gelu_ok, 3 * s + 1 + 3)
                        pairs = [(rg_hi[:, g, where[o, t]:where[o, t] + P], rg_lo[:, g, where[o, t]:where[o, t] + P],
                                  conv_hi[:, t, :], conv_lo[:, t, :]) for t in ins_t]
                        products(bank[:, b, :], pairs).then_inc(rg_done, 1)

            with pe.Fori(0, 2) as i:
                for half in range(2):
                    s = 2 * i + half
                    for j in range(3):
                        pe.wait_ge(gates_ok, 6 * s + 2 * j + 1)
                        cols_unit(Unit(U_LRU, 6 * half + j, i, 12), j, half == 0 and j == 0)
                    for j in range(3):
                        pe.wait_ge(gelu_ok, 3 * s + j + 1)
                        if j == 0:
                            pe.wait_ge(gates_ok, 6 * s + 6)
                        cols_unit(Unit(U_LRU, 6 * half + 3 + j, i, 12), 3 + j)
                    rg_tiles(s)
            for k in range(KD):
                if k < 2:
                    pe.wait_ge(gelu_ok, 12 + 3)
                else:
                    pe.wait_ge(grec_ok, k - 1)
                cols_unit(Unit(U_GREC, k), 4 + k % 2)
            pe.wait_ge(lru_split, WT + 3)
            pe.wait_ge(gates_ok, 24 + 6)
            with pe.Fori(0, 4) as i:
                for cc in range(2):
                    pe.wait_ge(lo_ok, 2 * i + cc + 1)
                    for j in range(2):
                        u = Unit(U_LO, 2 * cc + j, i, 4)
                        ready(u)
                        products(bank[:, cc, :], [(w_hi[:, u.slot, P * k:P * k + P], w_lo[:, u.slot, P * k:P * k + P],
                                                   lru_hi[:, 6 * j + k, :], lru_lo[:, 6 * j + k, :]) for k in range(6)],
                                 j == 0, j == 1).then_inc(units_done, 1)
            pe.wait_ge(lo_ok, 8 + 2)
            pe.wait_ge(grec_ok, KD)

            def pe_qk(h, u, ret=None):
                for j in range(4):
                    if j == 3 and ret is not None:
                        turn(ret)
                    pe.wait_ge(normed_ok, 4 * h + j + 1)
                    cols_unit(u.ahead(j), j)

            def turn(h):
                pe.wait_ge(normed_ok, 4 * h + 8)
                for j in range(4):
                    pe.wait_ge(silu_ok, 4 * h + j + 1)
                    for t in range(TT):
                        last = pe.transpose(bank[:, 4 + j, P * t:P * t + P], normed[:, t, P * j:P * j + P], ident[:, :])
                    last.then_inc(turned, 1)

            def pe_vg(h, u):
                for m in range(4):
                    ready(u.ahead(m))
                    slot = u.ahead(m).slot
                    for t in range(TT):
                        if m == 0:
                            pe.wait_ge(ret_out, 8 * h + 4 + t + 1)
                        last = products(bank[:, 4 + t, :], [
                            (xt_hi[:, 2 * m + k, P * t:P * t + P], xt_lo[:, 2 * m + k, P * t:P * t + P],
                             w_hi[:, slot, DV * k:DV * k + DV], w_lo[:, slot, DV * k:DV * k + DV]) for k in range(2)], m == 0, m == 3)
                    last.then_inc(units_done, 1)
                pe.wait_ge(qk_split, 4 * h + 4)
                for c_ in range(TT):
                    q0 = P * c_
                    products(bank[:, c_, 0:TOKENS - q0], [(qk_hi[:, 2 + k, q0:q0 + P], qk_lo[:, 2 + k, q0:q0 + P],
                                                          qk_hi[:, k, q0:TOKENS], qk_lo[:, k, q0:TOKENS]) for k in range(2)]).then_inc(scored, 1)
                for j in range(4):
                    pe.wait_ge(v_split, 4 * h + j + 1)
                    cols_unit(u.ahead(4 + j), 4 + j)
                spans = [0, 512, 896, 1152]
                for t in range(TT):
                    pe.wait_ge(p_split, 4 * h + t + 1)
                    products(bank[:, t, :], [(p_hi[:, spans[k] + P * (t - k):spans[k] + P * (t - k) + P],
                                              p_lo[:, spans[k] + P * (t - k):spans[k] + P * (t - k) + P],
                                              v_hi[:, k, :], v_lo[:, k, :]) for k in range(t + 1)]).then_inc(pv_ok, 1)

            def pe_ret(h, u):
                pe.wait_ge(ret_split, 4 * h + 8)
                for j in range(4):
                    ready(u.ahead(j))
                    slot = u.ahead(j).slot
                    for k in (2 * j, 2 * j + 1):
                        if k >= 4:
                            pe.wait_ge(ret_out, 8 * h + k - 3 + 8)
                        last = products(bank[:, 4 + k % 4, :], [
                            (w_hi[:, slot, 256 * x + P * (k % 2):256 * x + P * (k % 2) + P],
                             w_lo[:, slot, 256 * x + P * (k % 2):256 * x + P * (k % 2) + P],
                             ret_hi[:, x, :], ret_lo[:, x, :]) for x in range(4)])
                    last.then_inc(units_done, 1)

            pe_qk(0, Unit(U_QK0))
            with pe.Fori(0, HEADS - 1) as h:
                pe_vg(h, Unit(U_HEAD, 0, h, 16))
                pe_qk(h + 1, Unit(U_HEAD, 8, h, 16), h)
                pe_ret(h, Unit(U_HEAD, 12, h, 16))
            pe_vg(HEADS - 1, Unit(U_LAST))
            for k in range(KD):
                if k == 4:
                    turn(HEADS - 1)
                pe.wait_ge(normed_ok, 4 * HEADS + 4 if k >= 3 else 4 * HEADS + k + 1)
                if k >= 4:
                    pe.wait_ge(gret_ok, k - 3)
                cols_unit(Unit(U_GRET, k), k % 4)
            pe_ret(HEADS - 1, Unit(U_RET3))

            def turn_x2(t):
                pe.wait_ge(x2_ok, t + 1)
                if t:
                    pe.wait_ge(x2t_ok, t)
                for k in range(KD):
                    last = pe.transpose(bank[:, 4 + k // 4, P * (k % 4):P * (k % 4) + P], x2[:, t, P * k:P * k + P], ident[:, :])
                last.then_inc(x2_turned, 1)

            def router(t):
                pe.wait_ge(x2t_ok, t + 1)
                pe.wait_ge(router_in, 64)
                for k in range(KD):
                    last = pe.matmul(bank[:, 6, 36 * t:36 * t + 36], x2_t[:, t % 2, P * k:P * k + P], w_rt[:, 36 * k:36 * k + 36],
                                     start=k == 0, stop=k == KD - 1)
                last.then_inc(routed, 1)

            pe.wait_ge(split_done, U_END + RING)
            pe.wait_ge(gret_ok, KD)
            for t in range(TT):
                if t >= 2:
                    pe.wait_ge(z_ok, 2 * t - 2)
                for k in range(KD):
                    if t == 0:
                        pe.wait_ge(mrg_split, k + 1)
                    for half in range(2):
                        last = products(bank[:, 2 * (t % 2) + half, :], [
                            (mrg_hi[:, k, P * t:P * t + P], mrg_lo[:, k, P * t:P * t + P],
                             wo_hi[:, k, 512 * half:512 * half + 512], wo_lo[:, k, 512 * half:512 * half + 512])], k == 0, k == KD - 1)
                last.then_inc(proj_ok, 1)
                if t:
                    if t == 1:
                        pe.wait_ge(ret_out, 8 * HEADS + 8)
                    if t >= 2:
                        router(t - 2)
                    turn_x2(t - 1)
            router(TT - 2)
            turn_x2(TT - 1)
            router(TT - 1)
            pe.wait_ge(members_ok, 1)
            for t in range(TT + 1):
                dst = bank[:, 7, 32 * t:32 * t + 32]
                for k in range(min(t + 1, TT)):
                    last = pe.matmul(dst, tri_bf[:, :] if k == t else ones_bf[:, :], mem_bf[:, 32 * k:32 * k + 32],
                                     start=k == 0, stop=k == min(t, TT - 1))
            last.then_inc(ranked, 1)
            pe.wait_ge(ovf_ok, 1)
            pe.transpose(bank[0:1, 7, 256:256 + P], ovf_col[:, :], ident[:, :]).then_inc(ovf_turned, 1)

            def turn_x(s, ahead=0):
                pe.wait_ge(xg_in, 16 * s + 16 * (1 + ahead))
                if not (isinstance(s, int) and s == 0):
                    pe.wait_ge(xe_split, s)
                pe.sem_inc(marks, 1)
                for k in range(KD):
                    last = pe.transpose(bank_x[:, k, 0:ROWS], xg[0:ROWS, P * k:P * k + P], ident[0:ROWS, 0:ROWS])
                last.then_inc(xe_turned, 1)

            def gate_up(s, u):
                pe.wait_ge(xe_split, s + 1)
                for b in range(2):
                    for half in range(2):
                        v = u.ahead(2 * b + half)
                        pe.wait_ge(m_split_ok, v.n + 1 + MRING)
                        sl = v.slot % MSPLIT
                        products(bank[:, b, :], [(xe_hi[:, 4 * half + k, :], xe_lo[:, 4 * half + k, :],
                                                  m_hi[:, sl, FE * k:FE * k + FE], m_lo[:, sl, FE * k:FE * k + FE]) for k in range(4)],
                                 half == 0, half == 1).then_inc(m_done, 1)

            def turn_h(s):
                pe.wait_ge(h_ok, s + 1)
                pe.sem_inc(marks, 1)
                for k in range(4):
                    last = pe.transpose(bank_h[:, k, 0:ROWS], h_sb[0:ROWS, P * k:P * k + P], ident[0:ROWS, 0:ROWS])
                last.then_inc(h_turned, 1)

            def down(s, u):
                pe.wait_ge(ht_split, s + 1)
                pe.wait_ge(y_ok, s + 1)
                for half in range(2):
                    v = u.ahead(half)
                    pe.wait_ge(m_split_ok, v.n + 1 + MRING)
                    sl = v.slot % MSPLIT
                    for b in range(2):
                        last = products(bank[:, 2 + b, :], [
                            (ht_hi[:, 2 * half + k, :], ht_lo[:, 2 * half + k, :],
                             m_hi[:, sl, 1024 * k + 512 * b:1024 * k + 512 * b + 512], m_lo[:, sl, 1024 * k + 512 * b:1024 * k + 512 * b + 512])
                            for k in range(2)], half == 0, half == 1)
                    last.then_inc(m_done, 1)

            turn_x(0)
            gate_up(0, Unit(0, ring=MRING))
            turn_x(1)
            turn_h(0)

            def pe_next(e, u):
                gate_up(e + 1, u)
                turn_x(e + 2)
                down(e, u.ahead(4))
                turn_h(e + 1)

            with pe.Fori(0, PAIRS) as i:
                for b in range(2):
                    pe_next(2 * i + b, Unit(4 + 6 * b, 0, i, 12, MRING))
            pe_next(EXPERTS - 2, Unit(4 + 12 * PAIRS, ring=MRING))
            down(EXPERTS - 1, Unit(M_LAST, ring=MRING))
            pe.wait_ge(ovf_ready, 1)
            n_over = pe.value_load(ovf_row[0:1, 32:33], min_val=0, max_val=MAX_OVERFLOW)
            with pe.If(n_over > 0):
                with pe.Fori(0, (MAX_OVERFLOW + 1) // 2) as i:
                    for b in range(2):
                        j = 2 * i + b
                        with pe.If(n_over > j):
                            u = Unit(M_END + 6 * b, 0, i, 12, MRING)
                            turn_x(j + (EXPERTS + 1), 1)
                            gate_up(j + EXPERTS + 1, u)
                            turn_h(j + EXPERTS)
                            down(j + EXPERTS, u.ahead(4))


_INS = ['x', 'w_in', 'b_merge', 'conv_w', 'conv_b', 'w_rg_r', 'b_rg_r', 'w_rg_i', 'b_rg_i', 'lru_lambda', 'w_ret_o',
        'w_lru_o', 'w_out', 'ln1_g', 'ln1_b', 'w_group', 'b_group', 'w_exp_router', 'b_exp_router', 'w_e_gate',
        'w_e_up', 'w_e_down', 'ln2_g', 'ln2_b']


def _tables():
    half = DK // 2
    inv = np.float32(10000.0) ** (-np.arange(half, dtype=np.float32) / np.float32(half))
    ang = np.arange(TOKENS, dtype=np.float32)[None, :] * inv[:, None]
    rope = np.stack([np.cos(ang), np.sin(ang)]).astype(np.float32)
    log_g = np.log1p(-(2.0 ** (-5.0 - np.arange(HEADS))))
    diff = np.arange(TOKENS)[None, :] - np.arange(P)[:, None]
    decay = np.where(diff >= 0, np.exp(log_g[:, None, None] * np.maximum(diff, 0)), 0.0) * DK ** -0.5
    return rope, decay.astype(np.float32)


def kernel(**inputs):
    import concourse.bacc as _bacc
    from concourse.bass_utils import run_bass_kernel_spmd as _run

    nc = _bacc.Bacc("TRN2", target_bir_lowering=False, num_devices=1)
    arrays, io = {}, {}
    rope, decay = _tables()
    given = {n: inputs[n] for n in _INS}
    given.update(rope=rope, decay=decay)
    for name, value in given.items():
        a = np.ascontiguousarray(value)
        arrays[f"in_{name}_dram"] = a
        io[name] = nc.dram_tensor(f"in_{name}_dram", a.shape, mybir.dt.from_np(a.dtype), kind="ExternalInput").ap()
    out = nc.dram_tensor("out_0_dram", (1, TOKENS, D), F32, kind="ExternalOutput").ap()
    layer(nc, io, out)
    r = _run(nc, [arrays], core_ids=[0])
    return r.results[0]["out_0_dram"]
```
